# Optimizing a Trainium2 kernel written in Bass

```python
import jax, jax.numpy as jnp
from jax import lax
import numpy as np
import math

D_MODEL = 1024
BATCH = 1
SEQ = 256
DEPTH = 1

CHUNK = 64
N_META = 16
Q_BLOCK = 128
EPS = 1e-6
GLA_HEADS = 4
GLA_DK = 64
GLA_DV = 128
GLA_GATE_RANK = 16
GLA_TAU = 16.0
GLA_QK = GLA_HEADS * GLA_DK
GLA_VW = GLA_HEADS * GLA_DV
MLA_HEADS = 4
MLA_Q_RANK = 256
MLA_KV_RANK = 128
MLA_NOPE = 128
MLA_ROPE = 64
MLA_V = 128
MLA_OUT = MLA_HEADS * MLA_V
ROPE_BASE = 10000.0
D_MIX = GLA_VW + MLA_OUT
IN_WIDTHS = (GLA_QK, GLA_QK, GLA_VW, GLA_VW, GLA_GATE_RANK, MLA_Q_RANK, MLA_KV_RANK, MLA_ROPE)
D_IN = sum(IN_WIDTHS)
N_GROUPS = 8
EXPERTS_PER_GROUP = 8
N_EXPERTS = N_GROUPS * EXPERTS_PER_GROUP
TOP_K = 2
D_EXPERT = 512
MOE_BLOCK = 128


def rmsnorm(x, gain):
    x32 = x.astype(jnp.float32)
    y = x32 * lax.rsqrt(jnp.mean(x32 * x32, axis=-1, keepdims=True) + EPS)
    return (y * gain.astype(jnp.float32)).astype(x.dtype)

def split_points():
    pts, acc = [], 0
    for w in IN_WIDTHS[:-1]:
        acc += w
        pts.append(acc)
    return pts

def chunk_ids(length):
    p = jnp.arange(length)
    return jnp.where(p < N_META, 0, 1 + (p - N_META) // CHUNK)

def rope_tables(length):
    pos = jnp.arange(length, dtype=jnp.float32)
    inv = ROPE_BASE ** (-jnp.arange(0, MLA_ROPE, 2, dtype=jnp.float32) / MLA_ROPE)
    ang = pos[:, None] * inv[None, :]
    return jnp.cos(ang), jnp.sin(ang)

def apply_rope(x, cos, sin):
    half = x.shape[-1] // 2
    x1, x2 = x[..., :half].astype(jnp.float32), x[..., half:].astype(jnp.float32)
    return jnp.concatenate([x1 * cos - x2 * sin, x2 * cos + x1 * sin], axis=-1).astype(x.dtype)

def gla_group(q, k, v, r, a_low, w_a2, b_a, out_gain):
    f32 = jnp.float32
    B, L, _ = q.shape
    pad = (-L) % CHUNK
    log_a = jax.nn.log_sigmoid((a_low @ w_a2 + b_a).astype(f32)) / GLA_TAU

    def prep(t, d):
        t = jnp.pad(t.astype(f32), ((0, 0), (pad, 0), (0, 0)))
        n = t.shape[1] // CHUNK
        return t.reshape(B, n, CHUNK, GLA_HEADS, d).transpose(0, 3, 1, 2, 4)

    qc = prep(q, GLA_DK) * (GLA_DK ** -0.5)
    kc = prep(k, GLA_DK)
    vc = prep(v, GLA_DV)
    b = jnp.cumsum(prep(log_a, GLA_DK), axis=3)
    b_last = b[:, :, :, -1:, :]
    q_e = qc * jnp.exp(b)
    causal = jnp.tril(jnp.ones((CHUNK, CHUNK), dtype=bool))
    att = jnp.where(causal, jnp.einsum('bhncd,bhnsd->bhncs', q_e, kc * jnp.exp(-b)), 0.0)
    o = jnp.einsum('bhncs,bhnse->bhnce', att, vc)
    upd = jnp.einsum('bhncd,bhnce->nbhde', kc * jnp.exp(b_last - b), vc)
    decay = jnp.exp(b_last[:, :, :, 0, :]).transpose(2, 0, 1, 3)

    def step(s, inp):
        dec, u = inp
        return dec[..., None] * s + u, s

    s0 = jnp.zeros((B, GLA_HEADS, GLA_DK, GLA_DV), f32)
    _, s_prev = lax.scan(step, s0, (decay, upd))
    o = o + jnp.einsum('bhncd,nbhde->bhnce', q_e, s_prev)
    o = o.transpose(0, 2, 3, 1, 4).reshape(B, -1, GLA_HEADS, GLA_DV)[:, pad:]
    o = o * lax.rsqrt(jnp.mean(o * o, axis=-1, keepdims=True) + EPS)
    o = o.reshape(B, L, GLA_VW) * out_gain.astype(f32)
    return (o * jax.nn.silu(r.astype(f32))).astype(q.dtype)

def mla_group(q_lat, kv_lat, k_rope, q_norm, w_qb, kv_norm, w_kvb):
    B, L, _ = q_lat.shape
    q = (rmsnorm(q_lat, q_norm) @ w_qb).reshape(B, L, MLA_HEADS, MLA_NOPE + MLA_ROPE)
    q_nope, q_rope = q[..., :MLA_NOPE], q[..., MLA_NOPE:]
    kv = (rmsnorm(kv_lat, kv_norm) @ w_kvb).reshape(B, L, MLA_HEADS, MLA_NOPE + MLA_V)
    k_nope, v = kv[..., :MLA_NOPE], kv[..., MLA_NOPE:]
    cos, sin = rope_tables(L)
    q_rope = apply_rope(q_rope, cos[:, None, :], sin[:, None, :])
    k_rope = apply_rope(k_rope, cos, sin)
    key_chunk = chunk_ids(L)
    scale = (MLA_NOPE + MLA_ROPE) ** -0.5

    def attend(args):
        qn, qr, qcid = args
        s = (jnp.einsum('bqhd,bkhd->bhqk', qn, k_nope)
             + jnp.einsum('bqhd,bkd->bhqk', qr, k_rope)).astype(jnp.float32) * scale
        s = jnp.where(key_chunk[None, None, None, :] <= qcid[None, None, :, None], s, -jnp.inf)
        p = jax.nn.softmax(s, axis=-1).astype(v.dtype)
        return jnp.einsum('bhqk,bkhd->bqhd', p, v)

    meta_out = attend((q_nope[:, :N_META], q_rope[:, :N_META], key_chunk[:N_META]))
    nb = (L - N_META) // Q_BLOCK

    def blocks(t):
        return t[:, N_META:].reshape(B, nb, Q_BLOCK, *t.shape[2:]).swapaxes(0, 1)

    blk = lax.map(attend, (blocks(q_nope), blocks(q_rope), key_chunk[N_META:].reshape(nb, Q_BLOCK)))
    blk = blk.swapaxes(0, 1).reshape(B, L - N_META, MLA_HEADS, MLA_V)
    return jnp.concatenate([meta_out, blk], axis=1).reshape(B, L, MLA_OUT)

def hier_moe(u, wg, bg, we, be, w_gate, w_up, w_down):
    f32 = jnp.float32
    B, L, D = u.shape
    t = u.reshape(-1, D)
    n_tok = t.shape[0]
    g_prob = jax.nn.softmax((t @ wg + bg).astype(f32), axis=-1)
    g_p, g_idx = lax.top_k(g_prob, 1)
    e_logits = (t @ we + be).astype(f32).reshape(n_tok, N_GROUPS, EXPERTS_PER_GROUP)
    e_logits = jnp.take_along_axis(e_logits, g_idx[:, :, None], axis=1)[:, 0]
    e_p, e_idx = lax.top_k(jax.nn.softmax(e_logits, axis=-1), TOP_K)
    gates = g_p * e_p / jnp.sum(e_p, axis=-1, keepdims=True)
    expert = g_idx * EXPERTS_PER_GROUP + e_idx
    e_flat = expert.reshape(-1)
    tok_flat = jnp.repeat(jnp.arange(n_tok, dtype=jnp.int32), TOP_K)
    gate_flat = gates.reshape(-1)
    order = jnp.argsort(e_flat)
    e_sorted, tok_sorted, gate_sorted = e_flat[order], tok_flat[order], gate_flat[order]
    counts = jnp.bincount(e_flat, length=N_EXPERTS)
    padded = (counts + MOE_BLOCK - 1) // MOE_BLOCK * MOE_BLOCK
    pad_end = jnp.cumsum(padded)
    pad_start = pad_end - padded
    seg_start = jnp.cumsum(counts) - counts
    n_assign = n_tok * TOP_K
    dest = pad_start[e_sorted] + jnp.arange(n_assign) - seg_start[e_sorted]
    n_blocks = -(-(n_assign + N_EXPERTS * (MOE_BLOCK - 1)) // MOE_BLOCK)
    n_slots = n_blocks * MOE_BLOCK
    slot_tok = jnp.full((n_slots,), n_tok, jnp.int32).at[dest].set(tok_sorted)
    slot_gate = jnp.zeros((n_slots,), f32).at[dest].set(gate_sorted)
    block_expert = jnp.minimum(
        jnp.searchsorted(pad_end, jnp.arange(n_blocks) * MOE_BLOCK, side='right'), N_EXPERTS - 1)
    t_pad = jnp.concatenate([t, jnp.zeros((1, D), t.dtype)], axis=0)
    xs = t_pad[slot_tok].reshape(n_blocks, MOE_BLOCK, D)

    def expert_block(args):
        xb, e = args
        hdn = jax.nn.silu(xb @ w_gate[e]) * (xb @ w_up[e])
        return hdn @ w_down[e]

    ys = lax.map(expert_block, (xs, block_expert)).reshape(n_slots, D)
    out = jnp.zeros((n_tok + 1, D), f32).at[slot_tok].add(ys.astype(f32) * slot_gate[:, None])[:n_tok]
    return out.reshape(B, L, D).astype(u.dtype)

def first_inputs(seed: int = 0) -> dict:
    key = jax.random.key(seed)
    ks = jax.random.split(key, 24)
    f32 = jnp.float32

    def nrm(k, shape, scale):
        return jax.random.normal(k, shape, f32) * scale

    def gain(k, shape):
        return 1.0 + 0.02 * jax.random.normal(k, shape, f32)

    return {
        'x': nrm(ks[0], (BATCH, SEQ, D_MODEL), 1.0),
        'meta_tokens': nrm(ks[1], (N_META, D_MODEL), 1.0),
        'mix_norm': gain(ks[2], (DEPTH, D_MODEL)),
        'w_in': nrm(ks[3], (DEPTH, D_MODEL, D_IN), D_MODEL ** -0.5),
        'gla_w_a2': nrm(ks[4], (DEPTH, GLA_GATE_RANK, GLA_QK), GLA_GATE_RANK ** -0.5),
        'gla_b_a': nrm(ks[5], (DEPTH, GLA_QK), 0.1),
        'gla_out_norm': gain(ks[6], (DEPTH, GLA_VW)),
        'mla_q_norm': gain(ks[7], (DEPTH, MLA_Q_RANK)),
        'mla_w_qb': nrm(ks[8], (DEPTH, MLA_Q_RANK, MLA_HEADS * (MLA_NOPE + MLA_ROPE)), MLA_Q_RANK ** -0.5),
        'mla_kv_norm': gain(ks[9], (DEPTH, MLA_KV_RANK)),
        'mla_w_kvb': nrm(ks[10], (DEPTH, MLA_KV_RANK, MLA_HEADS * (MLA_NOPE + MLA_V)), MLA_KV_RANK ** -0.5),
        'w_out': nrm(ks[11], (DEPTH, D_MIX, D_MODEL), D_MIX ** -0.5),
        'ffn_norm': gain(ks[12], (DEPTH, D_MODEL)),
        'router_group_w': nrm(ks[13], (DEPTH, D_MODEL, N_GROUPS), D_MODEL ** -0.5),
        'router_group_b': nrm(ks[14], (DEPTH, N_GROUPS), 0.01),
        'router_expert_w': nrm(ks[15], (DEPTH, D_MODEL, N_EXPERTS), D_MODEL ** -0.5),
        'router_expert_b': nrm(ks[16], (DEPTH, N_EXPERTS), 0.01),
        'expert_w_gate': nrm(ks[17], (DEPTH, N_EXPERTS, D_MODEL, D_EXPERT), D_MODEL ** -0.5),
        'expert_w_up': nrm(ks[18], (DEPTH, N_EXPERTS, D_MODEL, D_EXPERT), D_MODEL ** -0.5),
        'expert_w_down': nrm(ks[19], (DEPTH, N_EXPERTS, D_EXPERT, D_MODEL), D_EXPERT ** -0.5),
        'final_norm': gain(ks[20], (D_MODEL,)),
    }

def first_block(x, meta_tokens, mix_norm, w_in, gla_w_a2, gla_b_a, gla_out_norm, mla_q_norm, mla_w_qb,
              mla_kv_norm, mla_w_kvb, w_out, ffn_norm, router_group_w, router_group_b, router_expert_w,
              router_expert_b, expert_w_gate, expert_w_up, expert_w_down, final_norm):
    B = x.shape[0]
    meta = jnp.broadcast_to(meta_tokens[None].astype(x.dtype), (B, N_META, x.shape[-1]))
    h = jnp.concatenate([meta, x], axis=1)
    pts = split_points()
    for l in range(DEPTH):
        u = rmsnorm(h, mix_norm[l])
        z = u @ w_in[l]
        q, k, v, r, a_low, q_lat, kv_lat, k_rope = jnp.split(z, pts, axis=-1)
        y_gla = gla_group(q, k, v, r, a_low, gla_w_a2[l], gla_b_a[l], gla_out_norm[l])
        y_mla = mla_group(q_lat, kv_lat, k_rope, mla_q_norm[l], mla_w_qb[l], mla_kv_norm[l], mla_w_kvb[l])
        h = h + jnp.concatenate([y_gla, y_mla], axis=-1) @ w_out[l]
        h = h + hier_moe(rmsnorm(h, ffn_norm[l]), router_group_w[l], router_group_b[l], router_expert_w[l],
                         router_expert_b[l], expert_w_gate[l], expert_w_up[l], expert_w_down[l])
    return rmsnorm(h, final_norm)[:, N_META:]


DEPTH_2 = 2

N_MEM = 256
N_MIXERS = 2
D_MIX_2 = D_MODEL
XA_HEADS = 4
XA_HEAD_DIM = D_MODEL // 16
D_XA = XA_HEADS * XA_HEAD_DIM
D_TOK = D_MIX_2 - D_XA
CONV_WIDTH = 3
ML_HEADS = 4
ML_HEAD_DIM = D_TOK // ML_HEADS
ML_CHUNK = 64
QK_CONV_WIDTH = 4
D_FF = 256 * int(math.ceil(8 * D_MODEL / 3 / 256))
LN_EPS = 1e-5
DEEPNORM_ALPHA = (2.0 * DEPTH_2) ** 0.25
DEEPNORM_BETA = (8.0 * DEPTH_2) ** -0.25
N_CONV_LAYERS = (DEPTH_2 + 1) // 2
N_MLSTM_LAYERS = DEPTH_2 // 2
D_IN_CONV = 3 * D_TOK + D_XA
D_IN_MLSTM = 4 * D_TOK + 2 * ML_HEADS + D_XA


def layer_norm(x, g, b):
    xf = x.astype(jnp.float32)
    mu = jnp.mean(xf, -1, keepdims=True)
    var = jnp.mean(jnp.square(xf - mu), -1, keepdims=True)
    y = (xf - mu) * lax.rsqrt(var + LN_EPS)
    return (y * g.astype(jnp.float32) + b.astype(jnp.float32)).astype(x.dtype)

def swiglu(x, w_gate, w_up, w_down):
    return (jax.nn.silu(x @ w_gate) * (x @ w_up)) @ w_down

def causal_dwconv(u, w):
    width = w.shape[0]
    s = u.shape[1]
    up = jnp.pad(u, ((0, 0), (width - 1, 0), (0, 0)))
    out = up[:, width - 1:width - 1 + s] * w[width - 1]
    for j in range(width - 1):
        out = out + up[:, j:j + s] * w[j]
    return out

def memory_cross_attention(q, mem_kv):
    b, s, _ = q.shape
    q = q.reshape(b, s, XA_HEADS, XA_HEAD_DIM)
    k, v = jnp.split(mem_kv, 2, -1)
    k = k.reshape(b, N_MEM, XA_HEADS, XA_HEAD_DIM)
    v = v.reshape(b, N_MEM, XA_HEADS, XA_HEAD_DIM)
    scores = jnp.einsum('bshd,bmhd->bhsm', q, k).astype(jnp.float32) * (XA_HEAD_DIM ** -0.5)
    p = jax.nn.softmax(scores, -1).astype(v.dtype)
    o = jnp.einsum('bhsm,bmhd->bshd', p, v)
    return o.reshape(b, s, D_XA)

def short_conv_mixer(u, conv_w):
    b_gate, c_gate, x_in = jnp.split(u, 3, -1)
    return b_gate * causal_dwconv(c_gate * x_in, conv_w)

def mlstm_chunkwise(q, k, v, log_i, log_f):
    b, s, _ = q.shape
    h_, dh, L = ML_HEADS, ML_HEAD_DIM, ML_CHUNK
    nc = s // L

    def to_chunks(t):
        return t.astype(jnp.float32).reshape(b, nc, L, h_, dh).transpose(1, 0, 3, 2, 4)

    def gate_chunks(g):
        return g.astype(jnp.float32).reshape(b, nc, L, h_).transpose(1, 0, 3, 2)

    qc, kc, vc = to_chunks(q), to_chunks(k) * (dh ** -0.5), to_chunks(v)
    ic, fc = gate_chunks(log_i), gate_chunks(log_f)
    causal = jnp.tril(jnp.ones((L, L), dtype=bool))

    def step(carry, xs):
        c_st, n_st, m_st = carry
        q_, k_, v_, li, lf = xs
        bcum = jnp.cumsum(lf, -1)
        log_d = bcum[..., :, None] - bcum[..., None, :] + li[..., None, :]
        log_d = jnp.where(causal, log_d, -jnp.inf)
        log_inter = bcum + m_st[..., None]
        m_t = jnp.maximum(log_inter, jnp.max(log_d, -1))
        w_intra = jnp.exp(log_d - m_t[..., None])
        w_inter = jnp.exp(log_inter - m_t)
        sc = jnp.einsum('bhtd,bhsd->bhts', q_, k_) * w_intra
        num = (jnp.einsum('bhts,bhse->bhte', sc, v_)
               + w_inter[..., None] * jnp.einsum('bhtd,bhde->bhte', q_, c_st))
        den = jnp.sum(sc, -1) + w_inter * jnp.einsum('bhtd,bhd->bht', q_, n_st)
        h = num / jnp.maximum(jnp.abs(den), jnp.exp(-m_t))[..., None]
        b_last = bcum[..., -1]
        log_w = b_last[..., None] - bcum + li
        m_new = jnp.maximum(b_last + m_st, jnp.max(log_w, -1))
        w_k = jnp.exp(log_w - m_new[..., None])
        decay = jnp.exp(b_last + m_st - m_new)
        c_new = decay[..., None, None] * c_st + jnp.einsum('bhs,bhsd,bhse->bhde', w_k, k_, v_)
        n_new = decay[..., None] * n_st + jnp.einsum('bhs,bhsd->bhd', w_k, k_)
        return (c_new, n_new, m_new), h

    init = (jnp.zeros((b, h_, dh, dh), jnp.float32),
            jnp.zeros((b, h_, dh), jnp.float32),
            jnp.zeros((b, h_), jnp.float32))
    _, hs = lax.scan(step, init, (qc, kc, vc, ic, fc))
    return hs.transpose(1, 0, 3, 2, 4).reshape(b, s, h_, dh)

def mlstm_mixer(u, b_gates, qk_conv_w, head_norm_g):
    b, s, _ = u.shape
    qk, v, o_pre, gates = jnp.split(u, [2 * D_TOK, 3 * D_TOK, 4 * D_TOK], -1)
    qk = jax.nn.silu(causal_dwconv(qk, qk_conv_w))
    q, k = jnp.split(qk, 2, -1)
    gates = gates.astype(jnp.float32) + b_gates.astype(jnp.float32)
    log_i = gates[..., :ML_HEADS]
    log_f = jax.nn.log_sigmoid(gates[..., ML_HEADS:])
    h = mlstm_chunkwise(q, k, v, log_i, log_f)
    mu = jnp.mean(h, -1, keepdims=True)
    var = jnp.mean(jnp.square(h - mu), -1, keepdims=True)
    h = (h - mu) * lax.rsqrt(var + LN_EPS) * head_norm_g.astype(jnp.float32)
    return jax.nn.sigmoid(o_pre) * h.reshape(b, s, D_TOK).astype(u.dtype)

def second_inputs(seed: int = 0) -> dict:
    key = jax.random.key(seed)
    ks = jax.random.split(key, 20)
    nrm = jax.random.normal
    f32 = jnp.float32
    x = nrm(ks[0], (BATCH, SEQ, D_MODEL), f32)
    mem = nrm(ks[1], (BATCH, N_MEM, D_MODEL), f32)
    ln_g = 1.0 + 0.02 * nrm(ks[2], (DEPTH_2, 3, D_MODEL), f32)
    ln_b = 0.02 * nrm(ks[3], (DEPTH_2, 3, D_MODEL), f32)
    ffn_w_gate = nrm(ks[4], (DEPTH_2, 2, D_MODEL, D_FF), f32) * D_MODEL ** -0.5
    ffn_w_up = nrm(ks[5], (DEPTH_2, 2, D_MODEL, D_FF), f32) * D_MODEL ** -0.5
    ffn_w_down = nrm(ks[6], (DEPTH_2, 2, D_FF, D_MODEL), f32) * (D_FF ** -0.5 * DEEPNORM_BETA)
    w_kv_mem = nrm(ks[7], (DEPTH_2, D_MODEL, 2 * D_XA), f32) * D_MODEL ** -0.5
    w_out = nrm(ks[8], (DEPTH_2, D_MIX_2, D_MODEL), f32) * (D_MIX_2 ** -0.5 * DEEPNORM_BETA)
    w_in_conv = nrm(ks[9], (N_CONV_LAYERS, D_MODEL, D_IN_CONV), f32) * D_MODEL ** -0.5
    conv_w = nrm(ks[10], (N_CONV_LAYERS, CONV_WIDTH, D_TOK), f32) * CONV_WIDTH ** -0.5
    w_in_mlstm = nrm(ks[11], (N_MLSTM_LAYERS, D_MODEL, D_IN_MLSTM), f32) * D_MODEL ** -0.5
    w_in_mlstm = w_in_mlstm.at[:, :, 4 * D_TOK:4 * D_TOK + 2 * ML_HEADS].multiply(0.1)
    b_i = 0.1 * nrm(ks[12], (N_MLSTM_LAYERS, ML_HEADS), f32)
    b_f = jnp.linspace(3.0, 6.0, ML_HEADS, dtype=f32) + 0.1 * nrm(ks[13], (N_MLSTM_LAYERS, ML_HEADS), f32)
    b_gates = jnp.concatenate([b_i, b_f], -1)
    qk_conv_w = nrm(ks[14], (N_MLSTM_LAYERS, QK_CONV_WIDTH, 2 * D_TOK), f32) * QK_CONV_WIDTH ** -0.5
    head_norm_g = 1.0 + 0.02 * nrm(ks[15], (N_MLSTM_LAYERS, ML_HEADS, ML_HEAD_DIM), f32)
    return {"x": x, "mem": mem, "ln_g": ln_g, "ln_b": ln_b,
            "ffn_w_gate": ffn_w_gate, "ffn_w_up": ffn_w_up, "ffn_w_down": ffn_w_down,
            "w_kv_mem": w_kv_mem, "w_out": w_out,
            "w_in_conv": w_in_conv, "conv_w": conv_w,
            "w_in_mlstm": w_in_mlstm, "b_gates": b_gates,
            "qk_conv_w": qk_conv_w, "head_norm_g": head_norm_g}

def second_block(x, mem, ln_g, ln_b, ffn_w_gate, ffn_w_up, ffn_w_down, w_kv_mem, w_out,
              w_in_conv, conv_w, w_in_mlstm, b_gates, qk_conv_w, head_norm_g):
    alpha = DEEPNORM_ALPHA
    for l in range(DEPTH_2):
        x = layer_norm(alpha * x + 0.5 * swiglu(x, ffn_w_gate[l, 0], ffn_w_up[l, 0], ffn_w_down[l, 0]),
                       ln_g[l, 0], ln_b[l, 0])
        mem_kv = mem @ w_kv_mem[l]
        j = l // N_MIXERS
        if l % N_MIXERS == 0:
            u = x @ w_in_conv[j]
            tok = short_conv_mixer(u[..., :3 * D_TOK], conv_w[j])
        else:
            u = x @ w_in_mlstm[j]
            tok = mlstm_mixer(u[..., :4 * D_TOK + 2 * ML_HEADS], b_gates[j], qk_conv_w[j], head_norm_g[j])
        xa = memory_cross_attention(u[..., -D_XA:], mem_kv)
        mix = jnp.concatenate([tok, xa], -1) @ w_out[l]
        x = layer_norm(alpha * x + mix, ln_g[l, 1], ln_b[l, 1])
        x = layer_norm(alpha * x + 0.5 * swiglu(x, ffn_w_gate[l, 1], ffn_w_up[l, 1], ffn_w_down[l, 1]),
                       ln_g[l, 2], ln_b[l, 2])
    return x


def setup_inputs(seed=0):
    out = dict(first_inputs(seed))
    for name, value in second_inputs(seed + 1).items():
        if name != "x":
            out[name + "_2"] = value
    return out


def reference(
    x, meta_tokens, mix_norm, w_in, gla_w_a2, gla_b_a, gla_out_norm, mla_q_norm, mla_w_qb,
    mla_kv_norm, mla_w_kvb, w_out, ffn_norm, router_group_w, router_group_b, router_expert_w,
    router_expert_b, expert_w_gate, expert_w_up, expert_w_down, final_norm, mem_2, ln_g_2,
    ln_b_2, ffn_w_gate_2, ffn_w_up_2, ffn_w_down_2, w_kv_mem_2, w_out_2, w_in_conv_2, conv_w_2,
    w_in_mlstm_2, b_gates_2, qk_conv_w_2, head_norm_g_2,
):
    x = first_block(
        x, meta_tokens, mix_norm, w_in, gla_w_a2, gla_b_a, gla_out_norm, mla_q_norm, mla_w_qb,
        mla_kv_norm, mla_w_kvb, w_out, ffn_norm, router_group_w, router_group_b,
        router_expert_w, router_expert_b, expert_w_gate, expert_w_up, expert_w_down, final_norm,
    )
    return second_block(
        x, mem_2, ln_g_2, ln_b_2, ffn_w_gate_2, ffn_w_up_2, ffn_w_down_2, w_kv_mem_2, w_out_2,
        w_in_conv_2, conv_w_2, w_in_mlstm_2, b_gates_2, qk_conv_w_2, head_norm_g_2,
    )


_drawn_inputs = setup_inputs


def setup_inputs(seed=0):
    import zlib

    import numpy as np

    out = dict(_drawn_inputs(seed))
    spreads = {}
    factors = {'gla_out_norm': 17.936,
     'mla_q_norm': 5.203,
     'mla_kv_norm': 6.314,
     'router_group_b': 33.719,
     'router_expert_b': 21.985,
     'head_norm_g_2': 29.938,
     'gla_b_a': 3.688,
     'ffn_norm': 7.242}
    for name, (base, spread) in spreads.items():
        noise = np.random.default_rng([zlib.crc32(name.encode()), seed]).standard_normal(out[name].shape)
        drawn = base * np.exp(spread * noise) if base else spread * noise
        out[name] = __import__('jax').numpy.asarray(drawn.astype(out[name].dtype))
    for name, factor in factors.items():
        out[name] = (out[name] * factor).astype(out[name].dtype)
    return out
```

```python
import numpy as np
from contextlib import ExitStack

import concourse.bass as bass
from concourse import mybir

F32 = mybir.dt.float32
I32 = mybir.dt.int32
ALU = mybir.AluOpType
ACT = mybir.ActivationFunctionType
AX = mybir.AxisListType

P = 128
D = 1024
KD = D // P
S = 256
TT = S // P
META = 16
L = S + META
CH = 64
NCH = S // CH
EPS = 1e-6
LN_EPS = 1e-5
BIG = 1e30

GH, DK, DV = 4, 64, 128
RANK, TAU = 16, 16.0
MH, NOPE, ROPE, MV = 4, 128, 64, 128
QR, KVR = 256, 128
C_Q, C_K, C_V, C_R = 0, 256, 512, 1024
C_A, C_QL, C_KV, C_KR = 1536, 1552, 1808, 1936
D_IN = 2000

NG, EG, NE, DE = 8, 8, 64, 512
SLOT = 32
QUAD = P // SLOT
ASSIGN = S * 2
MAX_BLOCKS = NE + (ASSIGN - NE) // SLOT
QUADS = -(-MAX_BLOCKS // QUAD)
RANKS = S // SLOT

XH, XD = 4, 64
NM = 256
TOK = 768
HH, HD = 4, 192
FF = 2816
FC = 256
NFC = FF // FC
ALPHA = 4.0 ** 0.25
CW, QW = 3, 4


class Chain:

    def __init__(self, sem):
        self.sem, self.n = sem, 0

    def __call__(self, eng, ins):
        self.n += 1
        ins.then_inc(self.sem, 1)
        eng.wait_ge(self.sem, self.n)


class Kit:

    def __init__(self):
        self.tiles = {}

    def __getattr__(self, name):
        return self.tiles[name]


def mid(ap, n):
    return ap.unsqueeze(2).broadcast_to([ap.shape[0], ap.shape[1], n])


def rep(ap, n):
    return ap.unsqueeze(1).broadcast_to([ap.shape[0], n, ap.shape[1]])


def stage_constants(K):
    nc = K.nc
    with nc.Block() as block:

        @block.gpsimd
        def _(g):
            K.pc(g, g.memset(K.ident[:, :], 0.0))
            K.pc(g, g.affine_select(out=K.ident[:, :], in_=K.ident[:, :], compare_op=ALU.not_equal, fill=1.0,
                                    base=0, pattern=[[-1, P]], channel_multiplier=1))
            K.pc(g, g.memset(K.ones[:, :], 1.0))
            K.pc(g, g.affine_select(out=K.earlier[:, :], in_=K.ones[:, :], compare_op=ALU.is_gt, fill=0.0,
                                    base=0, pattern=[[1, P]], channel_multiplier=-1))
            K.pc(g, g.iota(K.iota_i[:, :], [[1, P]], base=0, channel_multiplier=0))
            K.pc(g, g.tensor_copy(K.iota[:, :], K.iota_i[:, :]))

        @block.vector
        def _(v):
            v.memset(K.ones4[:, :], 1.0)
            v.memset(K.eps[:, 0:1], EPS)
            v.memset(K.eps[:, 1:2], LN_EPS)
            v.memset(K.eps[:, 2:3], 1.0)


def stage_project(K, M):
    nc, ps, dram = K.nc, K.ps, K.dram
    sem = K.sem
    ld_x, ld_gain, ld_small = sem("ld_x"), sem("ld_gain"), M.ld_small
    ld_w = [sem(f"ld_w_in{n}") for n in range(4)]
    sumsq, root, u_ready, turned, ut_ready = (sem(n) for n in ("a_sumsq", "a_root", "a_u_ready", "a_turned", "a_ut_ready"))
    z_done, z_out = sem("a_z_done"), sem("a_z_out")
    h, hM, u, uM, uT, Wi = K.h, M.hM, K.u, M.uM, M.uT, M.Wi
    w_in = dram["w_in"][0].rearrange("(p k) n -> p k n", k=KD)
    WCUT = [0, C_V, C_A, D_IN]
    ORDER = [0, 2, 1]
    groups = [("q", 0), ("q", 1), ("k", 0), ("k", 1), ("kr", 0), ("al", 0), ("lat", 0), ("lat", 1), ("lat", 2),
              ("v", 0), ("v", 1), ("v", 2), ("r", 0), ("r", 1)]
    bank = lambda n: (5 + n) % 8

    with nc.Block() as block:

        @block.sync
        def _(sp):
            sp.dma_start(h[:, :, :], dram["x"][0].rearrange("(t p) d -> p t d", p=P)).then_inc(ld_x, 16)
            sp.dma_start(hM[:, :], dram["meta_tokens"]).then_inc(ld_x, 16)
            for n in ORDER:
                sp.dma_start(Wi[:, :, WCUT[n]:WCUT[n + 1]], w_in[:, :, WCUT[n]:WCUT[n + 1]]).then_inc(ld_w[n], 16)
            sp.dma_start(M.wout[:, :, :], dram["w_out"][0].rearrange("(k p) n -> p k n", p=P)).then_inc(M.ld_wout, 16)

        @block.scalar
        def _(a):
            a.dma_start(M.mixg[:, :], dram["mix_norm"][0].rearrange("(p k) -> p k", k=KD)).then_inc(ld_gain, 16)
            a.dma_start(M.wa2[:, :], dram["gla_w_a2"][0]).then_inc(ld_small, 16)
            a.dma_start(M.ba[:, :], dram["gla_b_a"][0].rearrange("(h d) -> d h", h=GH), allow_slow_non_contiguous=True).then_inc(ld_small, 16)
            a.dma_start(M.gg[:, :], dram["gla_out_norm"][0].partition_broadcast(CH)).then_inc(ld_small, 16)
            a.dma_start(M.qg[:, :], dram["mla_q_norm"][0].rearrange("(k p) -> p k", p=P), allow_slow_non_contiguous=True).then_inc(ld_small, 16)
            a.dma_start(M.kvg[:, :], dram["mla_kv_norm"].rearrange("a p -> p a"), allow_slow_non_contiguous=True).then_inc(ld_small, 16)
            a.dma_start(M.wqb[:, :, :], dram["mla_w_qb"][0].rearrange("(k p) n -> p k n", p=P)).then_inc(ld_small, 16)
            a.dma_start(M.wkvb[:, :], dram["mla_w_kvb"][0]).then_inc(ld_small, 16)
            a.dma_start(M.cos[:, :], dram["rope_cos"]).then_inc(ld_small, 16)
            a.dma_start(M.sin[:, :], dram["rope_sin"]).then_inc(ld_small, 16)
            a.dma_start(M.fng[:, :], dram["ffn_norm"][0].rearrange("(p k) -> p k", k=KD)).then_inc(ld_small, 16)
            a.dma_start(M.wr[:, :, 0:NG], dram["router_group_w"][0].rearrange("(p k) n -> p k n", k=KD)).then_inc(ld_small, 16)
            a.dma_start(M.wr[:, :, NG:NG + NE], dram["router_expert_w"][0].rearrange("(p k) n -> p k n", k=KD)).then_inc(ld_small, 16)
            a.dma_start(M.br[:, 0:NG], dram["router_group_b"][0].partition_broadcast(P)).then_inc(ld_small, 16)
            a.dma_start(M.br[:, NG:NG + NE], dram["router_expert_b"][0].partition_broadcast(P)).then_inc(ld_small, 16)
            a.wait_ge(ld_x, 32)
            for t in range(TT):
                K.ac(a, a.activation(M.junk[:, :], h[:, t, :], ACT.Square, accum_out=M.ss[:, t:t + 1]))
            K.ac(a, a.activation(M.junk[0:META, :], hM[:, :], ACT.Square, accum_out=M.ssM[:, 0:1]))
            a.activation(M.rs[:, 0:TT], M.ss[:, 0:TT], ACT.Sqrt, bias=K.eps[:, 0:1], scale=1.0 / D).then_inc(root, 1)
            a.activation(M.rsM[:, 0:1], M.ssM[:, 0:1], ACT.Sqrt, bias=K.eps[0:META, 0:1], scale=1.0 / D).then_inc(root, 1)
            for n, (kind, i) in enumerate(groups):
                src = ps[:, bank(n), :]
                a.wait_ge(z_done, n + 1)
                if kind in "qk":
                    dst, sc = (M.qT, DK ** -0.5) if kind == "q" else (M.kT, 1.0)
                    a.activation(dst[:, 2 * i, :], src[0:64, 0:L], ACT.Copy, scale=sc)
                    a.activation(dst[:, 2 * i + 1, :], src[64:128, 0:L], ACT.Copy, scale=sc).then_inc(z_out, 1)
                elif kind == "kr":
                    a.activation(M.krT[:, :], src[0:ROPE, 0:L], ACT.Copy).then_inc(z_out, 1)
                elif kind == "al":
                    a.activation(M.alT[:, :], src[0:RANK, 0:L], ACT.Copy).then_inc(z_out, 1)
                elif kind == "lat" and i < TT:
                    a.activation(M.lat[:, i, :], src[:, 0:QR + KVR], ACT.Copy).then_inc(z_out, 1)
                elif kind == "lat":
                    a.activation(M.latM[:, :], src[0:META, 0:KVR], ACT.Copy).then_inc(z_out, 1)
                elif kind == "v" and i == TT:
                    a.activation(M.v[0:META, 0, :], src[0:META, :], ACT.Copy).then_inc(z_out, 1)
                elif kind == "v":
                    a.activation(M.v[:, 1 + 2 * i, :], src[0:64, :], ACT.Copy)
                    a.activation(M.v[:, 2 + 2 * i, :], src[64:128, :], ACT.Copy).then_inc(z_out, 1)
                else:
                    a.activation(M.r[:, 2 * i, :], src[0:64, :], ACT.Silu)
                    a.activation(M.r[:, 2 * i + 1, :], src[64:128, :], ACT.Silu).then_inc(z_out, 1)

        @block.vector
        def _(v):
            v.wait_ge(root, 2)
            K.vc(v, v.reciprocal(M.rs[:, 0:TT], M.rs[:, 0:TT]))
            K.vc(v, v.reciprocal(M.rsM[:, 0:1], M.rsM[:, 0:1]))
            for t in range(TT):
                v.tensor_scalar(u[:, t, :], h[:, t, :], M.rs[:, t:t + 1], None, ALU.mult).then_inc(u_ready, 1)
            v.tensor_scalar(uM[:, :], hM[:, :], M.rsM[:, 0:1], None, ALU.mult).then_inc(u_ready, 1)
            v.wait_ge(ld_gain, 16)
            for t in range(TT):
                for b in range(2):
                    v.wait_ge(turned, 2 * t + b + 1)
                    v.tensor_tensor(uT[:, 4 * b:4 * b + 4, t * P:(t + 1) * P],
                                    ps[:, 2 * t + b, :].rearrange("p (k n) -> p k n", k=4),
                                    mid(M.mixg[:, 4 * b:4 * b + 4], P), ALU.mult).then_inc(ut_ready, 1)
            v.wait_ge(turned, 5)
            v.tensor_tensor(uT[:, :, S:L], ps[:, 4, 0:KD * META].rearrange("p (k n) -> p k n", k=KD),
                            mid(M.mixg[:, :], META), ALU.mult).then_inc(ut_ready, 1)

        @block.tensor
        def _(pe):
            for t in range(TT):
                pe.wait_ge(u_ready, t + 1)
                for k in range(KD):
                    i = pe.transpose(ps[:, 2 * t + k // 4, (k % 4) * P:(k % 4 + 1) * P], u[:, t, k::KD], K.ident[:, :])
                    if k % 4 == 3:
                        i.then_inc(turned, 1)
            pe.wait_ge(u_ready, 3)
            for k in range(KD):
                i = pe.transpose(ps[:, 4, k * META:(k + 1) * META], uM[:, k::KD], K.ident[0:META, 0:META])
            i.then_inc(turned, 1)
            pe.wait_ge(ut_ready, 5)
            pe.wait_ge(ld_w[0], 16)
            for n, (kind, i) in enumerate(groups):
                if n >= 8:
                    pe.wait_ge(z_out, n - 7)
                if kind == "kr":
                    pe.wait_ge(ld_w[2], 16)
                if kind == "v":
                    pe.wait_ge(ld_w[1], 16)
                for k in range(KD):
                    if kind in ("q", "k", "kr", "al"):
                        c, m = {"q": (C_Q + i * P, P), "k": (C_K + i * P, P), "kr": (C_KR, ROPE), "al": (C_A, RANK)}[kind]
                        o, a, b = ps[0:m, bank(n), 0:L], Wi[:, k, c:c + m], uT[:, k, :]
                    else:
                        c, w = {"lat": (C_QL, QR + KVR), "v": (C_V, 512), "r": (C_R, 512)}[kind]
                        m = P if i < TT else META
                        if kind == "lat" and i == TT:
                            c, w = C_KV, KVR
                        o, a, b = ps[0:m, bank(n), 0:w], uT[:, k, i * P:i * P + m], Wi[:, k, c:c + w]
                    mm = pe.matmul(o, a, b, start=(k == 0), stop=(k == KD - 1))
                mm.then_inc(z_done, 1)


def stage_gla(K, M):
    nc, ps, sem = K.nc, K.ps, K.sem
    names = ("gate_mm", "gate_x", "gate_na", "gate_l", "decay_b", "exps", "att_mm", "att_out", "att_masked", "prod",
             "kw_mm", "kw_out", "upd_mm", "state", "o_mm", "o_out", "o_root", "y_ready", "y_mm", "y_out")
    s = {n: sem("g_" + n) for n in names}
    x, e, l, b = M.gx, M.ge, M.gl, M.gb
    chunk = lambda t, c: t[:, :, S:L] if c == 0 else t[:, :, (c - 1) * CH:c * CH]
    tok = lambda c: META if c == 0 else CH

    with nc.Block() as block:

        @block.tensor
        def _(pe):
            pe.wait_ge(M.ld_small, 16 * M.n_small)
            for hh in range(GH):
                i = pe.matmul(ps[0:DK, hh, 0:L], M.wa2[:, hh * DK:(hh + 1) * DK], M.alT[:, :], start=True, stop=True)
            i.then_inc(s["gate_mm"], 1)
            pe.wait_ge(s["prod"], 2)
            for c in range(NCH):
                for hh in range(GH):
                    n = c * GH + hh
                    i = pe.matmul(ps[0:CH, 4 + n // 8, (n % 8) * CH:(n % 8 + 1) * CH],
                                  M.ke[:, hh, c * CH:(c + 1) * CH], M.qe[:, hh, c * CH:(c + 1) * CH], start=True, stop=True)
            i.then_inc(s["att_mm"], 1)
            pe.wait_ge(s["prod"], 3)
            for c in range(NCH):
                for hh in range(GH):
                    n = c * GH + hh
                    i = pe.transpose(ps[0:tok(c), 6 + n // 8, (n % 8) * DK:(n % 8 + 1) * DK],
                                     chunk(M.kw, c)[:, hh, :], K.ident[0:DK, 0:DK])
            i.then_inc(s["kw_mm"], 1)
            pe.wait_ge(s["kw_out"], 2)
            for c in range(NCH):
                for hh in range(GH):
                    i = pe.matmul(ps[0:DK, c, hh * DV:(hh + 1) * DV], M.kwc[0:tok(c), c * GH + hh, :],
                                  M.v[0:tok(c), c, hh * DV:(hh + 1) * DV], start=True, stop=True)
                i.then_inc(s["upd_mm"], 1)
            pe.wait_ge(s["att_masked"], 1)
            for c in range(NCH):
                pe.wait_ge(s["state"], c + 1)
                for hh in range(GH):
                    o = ps[0:CH, 4 + c, hh * DV:(hh + 1) * DV]
                    pe.matmul(o, M.att[:, c * GH + hh, :], M.v[:, 1 + c, hh * DV:(hh + 1) * DV], start=True, stop=False)
                    i = pe.matmul(o, M.qe[:, hh, c * CH:(c + 1) * CH], M.st[:, c, hh, :], start=False, stop=True)
                i.then_inc(s["o_mm"], 1)
            pe.wait_ge(s["y_ready"], 1)
            for m in range(4):
                for c in range(NCH):
                    i = pe.transpose(ps[:, m // 2, (m % 2) * S + c * CH:(m % 2) * S + (c + 1) * CH],
                                     M.o[:, c, m * P:(m + 1) * P], K.ident[0:CH, 0:CH])
            i.then_inc(s["y_mm"], 1)

        @block.vector
        def _(v):
            v.wait_ge(s["gate_mm"], 1)
            v.wait_ge(M.ld_small, 16 * M.n_small)
            K.vc(v, v.tensor_tensor(x[:, :, :], ps[0:DK, 0:GH, 0:L], mid(M.ba[:, :], L), ALU.add))
            v.scalar_tensor_tensor(out=e[:, :, :], in0=x[:, :, :], scalar=-1.0, in1=x[:, :, :],
                                   op0=ALU.mult, op1=ALU.min).then_inc(s["gate_na"], 1)
            K.vc(v, v.memset(M.keep[:, :, :], 1.0))
            K.vc(v, v.memset(M.keep[:, :, 0:S + 1:CH], 0.0))
            v.wait_ge(s["gate_l"], 1)
            K.vc(v, v.scalar_tensor_tensor(out=x[:, :, :], in0=x[:, :, :], scalar=0.0, in1=l[:, :, :],
                                           op0=ALU.min, op1=ALU.subtract))
            K.vc(v, v.tensor_tensor_scan(b[:, :, :].rearrange("p h t -> p (h t)"),
                                         M.keep[:, :, :].rearrange("p h t -> p (h t)"),
                                         x[:, :, :].rearrange("p h t -> p (h t)"), 0.0, ALU.mult, ALU.add))
            for hh in range(GH):
                bx = b[:, hh, 0:S].rearrange("p (c t) -> p c t", c=NCH)
                v.tensor_tensor(x[:, hh, 0:S].rearrange("p (c t) -> p c t", c=NCH),
                                mid(b[:, hh, CH - 1:S:CH], CH), bx, ALU.subtract)
            v.tensor_tensor(x[:, :, S:L], b[:, :, L - 1:L].broadcast_to([DK, GH, META]), b[:, :, S:L],
                            ALU.subtract).then_inc(s["decay_b"], 1)
            v.wait_ge(s["exps"], 1)
            v.tensor_tensor(M.qe[:, :, :], M.qT[:, :, 0:S], M.eb[:, :, 0:S], ALU.mult).then_inc(s["prod"], 1)
            v.wait_ge(s["exps"], 2)
            v.tensor_tensor(M.ke[:, :, :], M.kT[:, :, 0:S], M.enb[:, :, 0:S], ALU.mult).then_inc(s["prod"], 1)
            v.wait_ge(s["exps"], 3)
            v.tensor_tensor(M.kw[:, :, :], M.kT[:, :, :], M.ekb[:, :, :], ALU.mult).then_inc(s["prod"], 1)
            v.wait_ge(s["att_mm"], 1)
            v.tensor_copy(M.att[:, :, :], ps[0:CH, 4:6, :].rearrange("p b (n t) -> p (b n) t", t=CH)).then_inc(s["att_out"], 1)
            v.wait_ge(s["upd_mm"], 1)
            v.tensor_copy(M.st[:, 0, :, :], ps[0:DK, 0, :].rearrange("p (h e) -> p h e", h=GH)).then_inc(s["state"], 1)
            v.wait_ge(s["exps"], 4)
            for c in range(1, NCH):
                v.wait_ge(s["upd_mm"], c + 1)
                v.wait_ge(s["state"], c)
                for hh in range(GH):
                    i = v.scalar_tensor_tensor(out=M.st[:, c, hh, :], in0=M.st[:, c - 1, hh, :],
                                               scalar=M.dec[:, hh, c:c + 1], in1=ps[0:DK, c, hh * DV:(hh + 1) * DV],
                                               op0=ALU.mult, op1=ALU.add)
                i.then_inc(s["state"], 1)
            for c in range(NCH):
                v.wait_ge(s["o_mm"], c + 1)
                v.tensor_copy(M.o[:, c, :], ps[0:CH, 4 + c, :]).then_inc(s["o_out"], 1)
            v.wait_ge(s["o_out"], NCH)
            oh = M.o[:, :, :].rearrange("p c (h e) -> p (c h) e", h=GH)
            K.vc(v, v.tensor_tensor(M.osq[:, :, :], oh, oh, ALU.mult))
            v.tensor_reduce(M.oss[:, :], M.osq[:, :, :], AX.X, ALU.add).then_inc(s["o_out"], 1)
            v.wait_ge(s["o_root"], 1)
            K.vc(v, v.reciprocal(M.oss[:, :], M.oss[:, :]))
            K.vc(v, v.tensor_tensor(oh, oh, mid(M.oss[:, :], DV), ALU.mult))
            K.vc(v, v.tensor_tensor(M.o[:, :, :], M.o[:, :, :], rep(M.gg[:, :], NCH), ALU.mult))
            v.tensor_tensor(M.o[:, :, :], M.o[:, :, :], M.r[:, :, :], ALU.mult).then_inc(s["y_ready"], 1)
            v.wait_ge(s["y_mm"], 1)
            v.tensor_copy(M.yT[:, 0:4, :], ps[:, 0:2, :].rearrange("p b (m t) -> p (b m) t", m=2)).then_inc(s["y_out"], 1)

        @block.scalar
        def _(a):
            a.wait_ge(s["gate_na"], 1)
            K.ac(a, a.activation(e[:, :, :], e[:, :, :], ACT.Exp))
            a.activation(l[:, :, :], e[:, :, :], ACT.Ln, bias=K.eps[0:DK, 2:3]).then_inc(s["gate_l"], 1)
            a.wait_ge(s["decay_b"], 1)
            a.activation(M.eb[:, :, :], b[:, :, :], ACT.Exp, scale=1.0 / TAU).then_inc(s["exps"], 1)
            a.activation(M.enb[:, :, :], b[:, :, :], ACT.Exp, scale=-1.0 / TAU).then_inc(s["exps"], 1)
            a.activation(M.ekb[:, :, :], x[:, :, :], ACT.Exp, scale=1.0 / TAU).then_inc(s["exps"], 1)
            a.activation(M.dec[:, :, 0:1], b[:, :, L - 1:L], ACT.Exp, scale=1.0 / TAU)
            a.activation(M.dec[:, :, 1:NCH + 1], b[:, :, CH - 1:S:CH], ACT.Exp, scale=1.0 / TAU).then_inc(s["exps"], 1)
            a.wait_ge(s["kw_mm"], 1)
            kwc = ps[:, 6:8, :].rearrange("p b (n d) -> p (b n) d", d=DK)
            a.activation(M.kwc[0:META, 0:GH, :], kwc[0:META, 0:GH, :], ACT.Copy).then_inc(s["kw_out"], 1)
            a.activation(M.kwc[:, GH:GH * NCH, :], kwc[0:CH, GH:GH * NCH, :], ACT.Copy).then_inc(s["kw_out"], 1)
            a.wait_ge(s["o_out"], NCH + 1)
            a.activation(M.oss[:, :], M.oss[:, :], ACT.Sqrt, bias=K.eps[0:CH, 0:1], scale=1.0 / DV).then_inc(s["o_root"], 1)

        @block.gpsimd
        def _(g):
            g.wait_ge(s["att_out"], 1)
            g.affine_select(out=M.att[:, :, :], in_=M.att[:, :, :], compare_op=ALU.is_ge, fill=0.0, base=0,
                            pattern=[[0, NCH * GH], [1, CH]], channel_multiplier=-1).then_inc(s["att_masked"], 1)


def stage_mla(K, M):
    nc, ps, sem = K.nc, K.ps, K.sem
    names = ("ss", "root", "norm", "lat_mm", "lat_out", "q_mm", "q_out", "kn_mm", "kn_out", "v_mm", "v_out", "rope_mm", "rope_out",
             "s_mm", "s_out", "max", "p", "pt_mm", "pt_out", "o_mm", "o_out", "y_mm", "y_out")
    s = {n: sem("m_" + n) for n in names}
    SC = float(NOPE + ROPE) ** -0.5
    PT = [(qt, hh, kt) for qt in range(TT) for hh in range(MH) for kt in range(qt + 1)]
    at = {x: n for n, x in enumerate(PT)}

    with nc.Block() as block:

        @block.scalar
        def _(a):
            for t in range(TT):
                K.ac(a, a.activation(M.junk[:, 0:QR], M.lat[:, t, 0:QR], ACT.Square, accum_out=M.lss[:, t:t + 1]))
                K.ac(a, a.activation(M.junk[:, 0:KVR], M.lat[:, t, QR:QR + KVR], ACT.Square,
                                     accum_out=M.lss[:, 2 + t:3 + t]))
            K.ac(a, a.activation(M.junk[0:META, 0:KVR], M.latM[:, :], ACT.Square, accum_out=M.lssM[:, 0:1]))
            a.activation(M.lss[:, 0:2], M.lss[:, 0:2], ACT.Sqrt, bias=K.eps[:, 0:1], scale=1.0 / QR)
            a.activation(M.lss[:, 2:4], M.lss[:, 2:4], ACT.Sqrt, bias=K.eps[:, 0:1], scale=1.0 / KVR)
            a.activation(M.lssM[:, :], M.lssM[:, :], ACT.Sqrt, bias=K.eps[0:META, 0:1], scale=1.0 / KVR).then_inc(s["root"], 1)
            a.wait_ge(s["kn_mm"], 1)
            a.activation(M.kn[:, :, :], ps[:, 4:8, 0:L], ACT.Copy).then_inc(s["kn_out"], 1)
            a.wait_ge(s["q_mm"], 1)
            a.activation(M.qn[:, :, :], ps[:, 0:2, :].rearrange("p b (h t) -> p (b h) t", h=2), ACT.Copy).then_inc(s["q_out"], 1)
            a.wait_ge(s["v_mm"], 1)
            a.activation(M.vv[:, :, :], ps[:, 4:6, :], ACT.Copy)
            a.activation(M.vvM[:, :], ps[0:META, 6, :], ACT.Copy).then_inc(s["v_out"], 1)
            a.wait_ge(s["max"], 1)
            for n in range(TT * MH):
                i = a.activation(M.sc[:, n, :], M.sc[:, n, :], ACT.Exp, bias=M.mx[:, n:n + 1], scale=SC,
                                 accum_out=M.rsum[:, n:n + 1])
                i.then_inc(s["p"], 1)

        @block.vector
        def _(v):
            v.wait_ge(s["root"], 1)
            K.vc(v, v.reciprocal(M.lss[:, :], M.lss[:, :]))
            K.vc(v, v.reciprocal(M.lssM[:, :], M.lssM[:, :]))
            for t in range(TT):
                v.tensor_scalar(M.lat[:, t, 0:QR], M.lat[:, t, 0:QR], M.lss[:, t:t + 1], None, ALU.mult)
                v.tensor_scalar(M.lat[:, t, QR:QR + KVR], M.lat[:, t, QR:QR + KVR], M.lss[:, 2 + t:3 + t], None, ALU.mult)
            v.tensor_scalar(M.latM[:, :], M.latM[:, :], M.lssM[:, 0:1], None, ALU.mult).then_inc(s["norm"], 1)
            v.wait_ge(s["lat_mm"], 1)
            v.tensor_tensor(M.qlT[:, :, :], ps[:, 0, :].rearrange("p (k t) -> p k t", k=2), mid(M.qg[:, :], S), ALU.mult)
            v.tensor_scalar(M.kvT[:, :], ps[:, 1, 0:L], M.kvg[:, 0:1], None, ALU.mult).then_inc(s["lat_out"], 1)
            HR = ROPE // 2
            K.vc(v, v.tensor_tensor(M.kr[:, :], M.krT[:, :], M.cos[:, :], ALU.mult))
            K.vc(v, v.tensor_tensor(M.rt[0:HR, 0, 0:L], M.krT[HR:ROPE, :], M.sin[HR:ROPE, :], ALU.mult))
            K.vc(v, v.tensor_tensor(M.rt[HR:ROPE, 0, 0:L], M.krT[0:HR, :], M.sin[0:HR, :], ALU.mult))
            K.vc(v, v.tensor_tensor(M.kr[:, :], M.kr[:, :], M.rt[:, 0, 0:L], ALU.add))
            v.wait_ge(s["rope_mm"], 1)
            qr = ps[:, 2:4, :].rearrange("p b (h t) -> p (b h) t", h=2)
            K.vc(v, v.tensor_tensor(M.qr[:, :, :], qr[0:ROPE], rep(M.cos[:, 0:S], MH), ALU.mult))
            K.vc(v, v.tensor_tensor(M.rt[0:HR, :, 0:S], qr[HR:ROPE], rep(M.sin[HR:ROPE, 0:S], MH), ALU.mult))
            K.vc(v, v.tensor_tensor(M.rt[HR:ROPE, :, 0:S], qr[0:HR], rep(M.sin[0:HR, 0:S], MH), ALU.mult))
            v.tensor_tensor(M.qr[:, :, :], M.qr[:, :, :], M.rt[:, :, 0:S], ALU.add).then_inc(s["rope_out"], 1)
            K.vc(v, v.memset(M.sc[:, :, :], -BIG))
            v.wait_ge(s["s_mm"], 1)
            for qt in range(TT):
                r = slice(MH * qt, MH * qt + MH)
                for half in range(2):
                    n = CH * (2 * qt + half + 1)
                    rows = slice(half * CH, half * CH + CH)
                    K.vc(v, v.tensor_copy(M.sc[rows, r, 0:n], ps[rows, r, 0:n]))
                K.vc(v, v.tensor_copy(M.sc[:, r, S:L], ps[:, r, S:L]))
            K.vc(v, v.tensor_reduce(M.mx[:, :], M.sc[:, :, :], AX.X, ALU.max))
            v.tensor_scalar(M.mx[:, :], M.mx[:, :], -SC, None, ALU.mult).then_inc(s["max"], 1)
            v.wait_ge(s["pt_mm"], 1)
            v.tensor_copy(M.pt[:, :, :], ps[:, 0:3, :].rearrange("p b (n t) -> p (b n) t", n=4))
            v.tensor_copy(M.ptM[:, :, :], ps[0:META, 3:5, :].rearrange("p b (n t) -> p (b n) t", n=4)).then_inc(s["pt_out"], 1)
            v.wait_ge(s["p"], TT * MH)
            K.vc(v, v.reciprocal(M.rsum[:, :], M.rsum[:, :]))
            v.wait_ge(s["o_mm"], 1)
            v.tensor_tensor(M.ym[:, :, :].rearrange("p t (h e) -> p (t h) e", h=MH),
                            ps[:, 5:7, :].rearrange("p t (h e) -> p (t h) e", h=MH),
                            mid(M.rsum[:, :], MV), ALU.mult).then_inc(s["o_out"], 1)
            v.wait_ge(s["y_mm"], 1)
            v.tensor_copy(M.yT[:, 4:8, :], ps[:, 0:2, :].rearrange("p b (m t) -> p (b m) t", m=2)).then_inc(s["y_out"], 1)

        @block.tensor
        def _(pe):
            pe.wait_ge(s["norm"], 1)
            for t in range(TT):
                for k in range(2):
                    pe.transpose(ps[:, 0, k * S + t * P:k * S + (t + 1) * P], M.lat[:, t, k * P:(k + 1) * P], K.ident[:, :])
                pe.transpose(ps[:, 1, t * P:(t + 1) * P], M.lat[:, t, QR:QR + KVR], K.ident[:, :])
            pe.transpose(ps[:, 1, S:L], M.latM[:, :], K.ident[0:META, 0:META]).then_inc(s["lat_mm"], 1)
            pe.wait_ge(s["lat_out"], 1)
            W = NOPE + MV
            for hh in range(MH):
                i = pe.matmul(ps[:, 4 + hh, 0:L], M.wkvb[:, hh * W:hh * W + NOPE], M.kvT[:, :], start=True, stop=True)
            i.then_inc(s["kn_mm"], 1)
            for hh in range(MH):
                for k in range(2):
                    i = pe.matmul(ps[0:ROPE, 2 + hh // 2, (hh % 2) * S:(hh % 2 + 1) * S],
                                  M.wqb[:, k, hh * 192 + NOPE:(hh + 1) * 192], M.qlT[:, k, :], start=(k == 0), stop=(k == 1))
            i.then_inc(s["rope_mm"], 1)
            for hh in range(MH):
                for k in range(2):
                    i = pe.matmul(ps[:, hh // 2, (hh % 2) * S:(hh % 2 + 1) * S],
                                  M.wqb[:, k, hh * 192:hh * 192 + NOPE], M.qlT[:, k, :], start=(k == 0), stop=(k == 1))
            i.then_inc(s["q_mm"], 1)
            pe.wait_ge(s["kn_out"], 1)
            wv = M.wkvb[:, :].rearrange("p (h n) -> p h n", h=MH)[:, :, NOPE:W]
            for t in range(TT):
                pe.matmul(ps[:, 4 + t, :], M.kvT[:, t * P:(t + 1) * P], wv, start=True, stop=True)
            pe.matmul(ps[0:META, 6, :], M.kvT[:, S:L], wv, start=True, stop=True).then_inc(s["v_mm"], 1)
            pe.wait_ge(s["q_out"], 1)
            pe.wait_ge(s["v_out"], 1)
            pe.wait_ge(s["rope_out"], 1)
            for qt in range(TT):
                for hh in range(MH):
                    o = ps[:, qt * MH + hh, 0:L]
                    pe.matmul(o, M.qn[:, hh, qt * P:(qt + 1) * P], M.kn[:, hh, :], start=True, stop=False)
                    i = pe.matmul(o, M.qr[:, hh, qt * P:(qt + 1) * P], M.kr[:, :], start=False, stop=True)
            i.then_inc(s["s_mm"], 1)
            pe.wait_ge(s["p"], TT * MH)
            for n, (qt, hh, kt) in enumerate(PT):
                pe.transpose(ps[:, n // 4, (n % 4) * P:(n % 4 + 1) * P], M.sc[:, qt * MH + hh, kt * P:(kt + 1) * P], K.ident[:, :])
            for n in range(TT * MH):
                i = pe.transpose(ps[0:META, 3 + n // 4, (n % 4) * P:(n % 4 + 1) * P], M.sc[:, n, S:L], K.ident[:, :])
            i.then_inc(s["pt_mm"], 1)
            pe.wait_ge(s["pt_out"], 1)
            for qt in range(TT):
                for hh in range(MH):
                    o = ps[:, 5 + qt, hh * MV:(hh + 1) * MV]
                    for kt in range(qt + 1):
                        pe.matmul(o, M.pt[:, at[qt, hh, kt], :], M.vv[:, kt, hh * MV:(hh + 1) * MV], start=(kt == 0), stop=False)
                    i = pe.matmul(o, M.ptM[:, qt * MH + hh, :], M.vvM[:, hh * MV:(hh + 1) * MV], start=False, stop=True)
            i.then_inc(s["o_mm"], 1)
            pe.wait_ge(s["o_out"], 1)
            for m in range(4):
                for t in range(TT):
                    i = pe.transpose(ps[:, m // 2, (m % 2) * S + t * P:(m % 2) * S + (t + 1) * P],
                                     M.ym[:, t, m * P:(m + 1) * P], K.ident[:, :])
            i.then_inc(s["y_mm"], 1)


def stage_route(K, M):
    nc, ps, sem = K.nc, K.ps, K.sem
    names = ("h_mm", "h_ready", "sumsq", "u_ready", "turned", "ut", "l_mm", "l_ready", "gexp_in", "gexp", "dexp_in",
             "dexp", "hot", "rank_mm", "cmp", "be_mm", "iota")
    s = {n: sem("r_" + n) for n in names}
    h, u = K.h, K.u
    G8 = lambda ap, n: ap.unsqueeze(2).broadcast_to([P, TT, n])

    with nc.Block() as block:

        @block.tensor
        def _(pe):
            pe.wait_ge(M.ld_wout, 16)
            for t in range(TT):
                for k in range(KD):
                    for n in range(2):
                        i = pe.matmul(ps[:, 2 * t + n, :], M.yT[:, k, t * P:(t + 1) * P], M.wout[:, k, n * 512:(n + 1) * 512],
                                      start=(k == 0), stop=(k == KD - 1))
                i.then_inc(s["h_mm"], 1)
            for t in range(TT):
                pe.wait_ge(s["u_ready"], t + 1)
                for k in range(KD):
                    i = pe.transpose(ps[:, 4 + 2 * t + k // 4, (k % 4) * P:(k % 4 + 1) * P], u[:, t, k::KD], K.ident[:, :])
                i.then_inc(s["turned"], 1)
            pe.wait_ge(s["ut"], 4)
            for t in range(TT):
                for k in range(KD):
                    i = pe.matmul(ps[:, t, 0:NG + NE], M.uT[:, k, t * P:(t + 1) * P], M.wr[:, k, :],
                                  start=(k == 0), stop=(k == KD - 1))
            i.then_inc(s["l_mm"], 1)
            pe.wait_ge(s["hot"], 1)
            pe.matmul(ps[:, 2, 0:NE], K.earlier[:, :], M.hot[:, 0, :], start=True, stop=True)
            pe.matmul(ps[:, 2, NE:2 * NE], K.earlier[:, :], M.hot[:, 1, :], start=True, stop=False)
            pe.matmul(ps[:, 2, NE:2 * NE], K.ones[:, :], M.hot[:, 0, :], start=False, stop=True)
            pe.matmul(ps[:, 2, 2 * NE:3 * NE], K.ones[:, :], M.hot[:, 0, :], start=True, stop=False)
            pe.matmul(ps[:, 2, 2 * NE:3 * NE], K.ones[:, :], M.hot[:, 1, :], start=False, stop=True).then_inc(s["rank_mm"], 1)
            pe.wait_ge(s["cmp"], 1)
            pe.matmul(ps[0:1, 3, 0:QUADS * QUAD], K.ones[0:NE, 0:1], M.cmp[:, :], start=True, stop=True).then_inc(s["be_mm"], 1)

        @block.scalar
        def _(a):
            for t in range(TT):
                a.wait_ge(s["h_ready"], t + 1)
                K.ac(a, a.activation(M.junk[:, :], h[:, t, :], ACT.Square, accum_out=M.ss[:, t:t + 1]))
            a.activation(M.rs[:, 0:TT], M.ss[:, 0:TT], ACT.Sqrt, bias=K.eps[:, 0:1], scale=1.0 / D).then_inc(s["sumsq"], 1)
            a.wait_ge(s["gexp_in"], 1)
            a.activation(M.ge8[:, :, :], M.ge8[:, :, :], ACT.Exp).then_inc(s["gexp"], 1)
            a.wait_ge(s["dexp_in"], 1)
            a.activation(M.ee[:, :], M.ee[:, :], ACT.Exp).then_inc(s["dexp"], 1)

        @block.gpsimd
        def _(g):
            K.pc(g, g.iota(M.i8i[:, :, :], [[0, TT], [1, EG]], base=-EG, channel_multiplier=0))
            K.pc(g, g.tensor_copy(M.i8[:, :, :], M.i8i[:, :, :]))
            K.pc(g, g.iota(M.i32i[:, :, :], [[0, NE], [SLOT, RANKS]], base=0, channel_multiplier=0))
            g.tensor_copy(M.i32[:, :, :], M.i32i[:, :, :]).then_inc(s["iota"], 1)

        @block.vector
        def _(v):
            c = lambda i: K.vc(v, i)
            for t in range(TT):
                v.wait_ge(s["h_mm"], t + 1)
                v.tensor_tensor(h[:, t, :], h[:, t, :], ps[:, 2 * t:2 * t + 2, :].rearrange("p b n -> p (b n)"),
                                ALU.add).then_inc(s["h_ready"], 1)
            v.wait_ge(s["sumsq"], 1)
            c(v.reciprocal(M.rs[:, 0:TT], M.rs[:, 0:TT]))
            for t in range(TT):
                v.tensor_scalar(u[:, t, :], h[:, t, :], M.rs[:, t:t + 1], None, ALU.mult).then_inc(s["u_ready"], 1)
            for t in range(TT):
                v.wait_ge(s["turned"], t + 1)
                for b in range(2):
                    v.tensor_tensor(M.uT[:, 4 * b:4 * b + 4, t * P:(t + 1) * P],
                                    ps[:, 4 + 2 * t + b, :].rearrange("p (k n) -> p k n", k=4),
                                    mid(M.fng[:, 4 * b:4 * b + 4], P), ALU.mult).then_inc(s["ut"], 1)
            v.wait_ge(s["l_mm"], 1)
            v.wait_ge(s["iota"], 1)
            c(v.tensor_tensor(M.lg[:, :, :], ps[:, 0:TT, 0:NG + NE], rep(M.br[:, :], TT), ALU.add))
            gl = M.lg[:, :, 0:NG]
            c(v.tensor_reduce(M.t0[:, :], gl, AX.X, ALU.max))
            v.tensor_tensor(M.ge8[:, :, :], gl, G8(M.t0[:, :], NG), ALU.subtract).then_inc(s["gexp_in"], 1)

            def first_hot(out, val, top):
                c(v.tensor_tensor(M.tmp8[:, :, :], val, G8(top, EG), ALU.is_ge))
                c(v.tensor_tensor(M.tmp8[:, :, :], M.tmp8[:, :, :], M.i8[:, :, :], ALU.mult))
                c(v.tensor_reduce(M.t1[:, :], M.tmp8[:, :, :], AX.X, ALU.min))
                c(v.tensor_tensor(out, M.i8[:, :, :], G8(M.t1[:, :], EG), ALU.is_equal))

            first_hot(M.gh[:, :, :], gl, M.t0[:, :])
            v.wait_ge(s["gexp"], 1)
            c(v.tensor_reduce(M.gp[:, :], M.ge8[:, :, :], AX.X, ALU.add))
            c(v.reciprocal(M.gp[:, :], M.gp[:, :]))
            for t in range(TT):
                c(v.tensor_tensor(M.e64[:, t, :].rearrange("p (g e) -> p g e", g=NG),
                                  M.lg[:, t, NG:NG + NE].rearrange("p (g e) -> p g e", g=NG),
                                  mid(M.gh[:, t, :], EG), ALU.mult))
                c(v.tensor_reduce(M.sel[:, t, :], M.e64[:, t, :].rearrange("p (g e) -> p e g", g=NG), AX.X, ALU.add))
            c(v.tensor_reduce(M.m1[:, :], M.sel[:, :, :], AX.X, ALU.max))
            first_hot(M.h1[:, :, :], M.sel[:, :, :], M.m1[:, :])
            c(v.scalar_tensor_tensor(out=M.sel[:, :, :], in0=M.h1[:, :, :], scalar=-BIG, in1=M.sel[:, :, :],
                                     op0=ALU.mult, op1=ALU.add))
            c(v.tensor_reduce(M.m2[:, :], M.sel[:, :, :], AX.X, ALU.max))
            first_hot(M.h2[:, :, :], M.sel[:, :, :], M.m2[:, :])
            v.tensor_tensor(M.ee[:, :], M.m2[:, :], M.m1[:, :], ALU.subtract).then_inc(s["dexp_in"], 1)
            v.wait_ge(s["dexp"], 1)
            c(v.tensor_scalar(M.t0[:, :], M.ee[:, :], 1.0, None, ALU.add))
            c(v.reciprocal(M.t0[:, :], M.t0[:, :]))
            c(v.tensor_tensor(K.gate[:, 0, :], M.gp[:, :], M.t0[:, :], ALU.mult))
            c(v.tensor_tensor(K.gate[:, 1, :], K.gate[:, 0, :], M.ee[:, :], ALU.mult))
            for t in range(TT):
                for dst, one in ((M.x1, M.h1), (M.x2, M.h2)):
                    c(v.tensor_tensor(dst[:, t, :].rearrange("p (g e) -> p g e", g=NG), mid(M.gh[:, t, :], EG),
                                      rep(one[:, t, :], NG), ALU.mult))
            v.tensor_tensor(M.hot[:, :, :], M.x1[:, :, :], M.x2[:, :, :], ALU.add).then_inc(s["hot"], 1)
            v.wait_ge(s["rank_mm"], 1)
            c(v.tensor_copy(M.cnt[:, :], ps[:, 2, 2 * NE:3 * NE]))
            c(v.tensor_tensor(M.gtm[:, :, :], mid(M.cnt[:, :], RANKS), M.i32[:, :, :], ALU.is_gt))
            c(v.tensor_reduce(M.nb[:, :], M.gtm[:, :, :], AX.X, ALU.add))
            c(v.tensor_tensor_scan(M.ends[:, :], K.ones[:, 0:NE], M.nb[:, :], 0.0, ALU.mult, ALU.add))
            c(v.tensor_tensor(M.e64[0:NE, 0, :], M.ends[0:NE, :], K.ident[0:NE, 0:NE], ALU.mult))
            c(v.tensor_reduce(M.ecol[:, :], M.e64[0:NE, 0, :], AX.X, ALU.add))
            v.tensor_scalar(M.cmp[:, :], K.iota[0:NE, 0:QUADS * QUAD], M.ecol[:, 0:1], None, ALU.is_ge).then_inc(s["cmp"], 1)
            c(v.tensor_tensor(M.nb[:, :], M.ends[:, :], M.nb[:, :], ALU.subtract))
            c(v.tensor_scalar(M.nb[:, :], M.nb[:, :], float(SLOT), None, ALU.mult))
            for t in range(TT):
                c(v.tensor_tensor(M.pos[:, t, :], ps[:, 2, t * NE:(t + 1) * NE], M.nb[:, :], ALU.add))
            for n, mark in ((0, M.x1), (1, M.x2)):
                c(v.tensor_tensor(mark[:, :, :], mark[:, :, :], M.pos[:, :, :], ALU.mult))
                c(v.tensor_reduce(K.slot[:, n, :], mark[:, :, :], AX.X, ALU.add))
            v.wait_ge(s["be_mm"], 1)
            v.tensor_scalar(K.table[:, 0:QUADS * QUAD], ps[0:1, 3, 0:QUADS * QUAD], float(NE - 1), None, ALU.min)
            v.tensor_copy(K.table[:, QUADS * QUAD:QUADS * QUAD + 1], M.ends[0:1, NE - 1:NE])


def stage_experts(K, E):
    nc, ps, sem, dram = K.nc, K.ps, K.sem, K.dram
    LOADS = [("gate", 0), ("up", 0), ("gate", 1), ("up", 1), ("down", 0), ("down", 1)]
    NL = len(LOADS)
    RING = 3
    arrived = [sem(f"e_arrived{n}") for n in range(RING)]
    free, select, turned_c, x_mm, x_out, gate_out, hid, h_mm, h_out, y_out, c_mm, summed = (
        sem("e_" + n) for n in ("free", "select", "turned_c", "x_mm", "x_out", "gate_out", "hid", "h_mm", "h_out",
                                "y_out", "c_mm", "summed"))
    ct_out = sem("e_ct_out")
    vs = sem("e_v_chain")
    wg = dram["expert_w_gate"][0].rearrange("e (p k) n -> e p (k n)", p=P)
    wu = dram["expert_w_up"][0].rearrange("e (p k) n -> e p (k n)", p=P)
    wd = dram["expert_w_down"][0].rearrange("e (p k) n -> e p (k n)", p=P)
    HALF = 4 * DE
    W = E.W

    def blocks_in_use(eng):
        return eng.value_load(K.table[0:1, QUADS * QUAD:QUADS * QUAD + 1], min_val=0, max_val=MAX_BLOCKS)

    with nc.Block() as block:

        @block.sync
        def _(sp):
            used = blocks_in_use(sp)
            with sp.Fori(0, QUADS) as q:
                with sp.If(used > q * QUAD):
                    ex = [sp.value_load(K.table[0:1, bass.ds(q * QUAD + j, 1)], min_val=0, max_val=NE - 1) for j in range(QUAD)]
                    for n, (kind, half) in enumerate(LOADS):
                        sp.wait_ge(free, q * NL + n + 1)
                        src = {"gate": wg, "up": wu, "down": wd}[kind]
                        for j in range(QUAD):
                            sp.dma_start(W[:, n % RING, j, :],
                                         src[bass.ds(ex[j], 1), :, half * HALF:(half + 1) * HALF].rearrange("a p n -> p (a n)"))\
                              .then_inc(arrived[n % RING], 16)

        @block.tensor
        def _(pe):
            for _i in range(RING):
                pe.sem_inc(free, 1)
            used = blocks_in_use(pe)
            with pe.Fori(0, QUADS) as q:
                with pe.If(used > q * QUAD):
                    pe.wait_ge(select, q + 1)
                    pe.wait_ge(summed, q + 1)
                    for k in range(KD):
                        for t in range(TT):
                            i = pe.matmul(ps[:, 4 + k // 4, (k % 4) * P:(k % 4 + 1) * P], K.u[:, t, k::KD], E.pick[:, t, :],
                                          start=(t == 0), stop=(t == TT - 1))
                    i.then_inc(x_mm, 1)
                    for t in range(TT):
                        i = pe.transpose(ps[:, 6, t * P:(t + 1) * P], E.mix[:, t, :], K.ident[:, :])
                    i.then_inc(turned_c, 1)
                    pe.wait_ge(x_out, 2 * q + 2)
                    for n in range(4):
                        pe.wait_ge(arrived[n % RING], q * 128 + (64 if n < RING else 128))
                        kind, half = LOADS[n]
                        b = 0 if kind == "gate" else 1
                        for k4 in range(4):
                            k = 4 * half + k4
                            for j in range(QUAD):
                                i = pe.matmul(ps[SLOT * j:SLOT * (j + 1), b, :], E.xT[:, k, SLOT * j:SLOT * (j + 1)],
                                              W[:, n % RING, j, k4 * DE:(k4 + 1) * DE], start=(k == 0), stop=(k == KD - 1))
                        i.then_inc(free, 1)
                    pe.wait_ge(hid, q + 1)
                    for f in range(4):
                        i = pe.transpose(ps[:, 7, f * P:(f + 1) * P], E.hid[:, f::4], K.ident[:, :])
                    i.then_inc(h_mm, 1)
                    pe.wait_ge(h_out, q + 1)
                    for n in range(4, NL):
                        pe.wait_ge(arrived[n % RING], q * 128 + 128)
                        for f2 in range(2):
                            f = 2 * (n - 4) + f2
                            for c in range(2):
                                for j in range(QUAD):
                                    i = pe.matmul(ps[SLOT * j:SLOT * (j + 1), 2 + c, :], E.hT[:, f, SLOT * j:SLOT * (j + 1)],
                                                  W[:, n % RING, j, f2 * D + c * 512:f2 * D + (c + 1) * 512],
                                                  start=(f == 0), stop=(f == 3))
                        i.then_inc(free, 1)
                    pe.wait_ge(y_out, q + 1)
                    for t in range(TT):
                        for c in range(2):
                            i = pe.matmul(ps[:, 4 + 2 * t + c, :], E.mixT[:, t, :], E.y[:, c * 512:(c + 1) * 512],
                                          start=True, stop=True)
                    i.then_inc(c_mm, 1)

        @block.scalar
        def _(a):
            used = blocks_in_use(a)
            with a.Fori(0, QUADS) as q:
                with a.If(used > q * QUAD):
                    a.wait_ge(turned_c, q + 1)
                    a.activation(E.mixT[:, :, :], ps[:, 6, 0:TT * P].rearrange("p (t n) -> p t n", t=TT), ACT.Copy).then_inc(ct_out, 1)
                    a.wait_ge(free, q * NL + RING + 4)
                    a.activation(E.act[:, :], ps[:, 0, :], ACT.Silu).then_inc(gate_out, 1)
                    a.wait_ge(h_mm, q + 1)
                    a.activation(E.hT[:, :, :], ps[:, 7, :].rearrange("p (f n) -> p f n", f=4), ACT.Copy).then_inc(h_out, 1)
                    a.wait_ge(free, q * NL + RING + 6)
                    a.wait_ge(ct_out, q + 1)
                    a.activation(E.y[:, :], ps[:, 2:4, :].rearrange("p b n -> p (b n)"), ACT.Copy).then_inc(y_out, 1)

        @block.vector
        def _(v):
            v.sem_inc(summed, 1)
            used = blocks_in_use(v)
            with v.Fori(0, QUADS) as q:
                with v.If(used > q * QUAD):
                    for t in range(TT):
                        v.tensor_scalar(E.one[:, 0, t, :], K.iota[:, :], K.slot[:, 0, t:t + 1], K.gate[:, 0, t:t + 1],
                                        ALU.is_equal, ALU.mult)
                        v.tensor_scalar(E.one[:, 1, t, :], K.iota[:, :], K.slot[:, 1, t:t + 1], K.gate[:, 1, t:t + 1],
                                        ALU.is_equal, ALU.mult)
                        v.tensor_scalar(E.one[:, 2, t, :], K.iota[:, :], K.slot[:, 0, t:t + 1], None, ALU.is_equal)
                        i = v.tensor_scalar(E.one[:, 3, t, :], K.iota[:, :], K.slot[:, 1, t:t + 1], None, ALU.is_equal)
                    i.then_inc(vs, 1)
                    v.wait_ge(vs, q * 2 + 1)
                    v.tensor_scalar(K.slot[:, :, :], K.slot[:, :, :], float(-P), None, ALU.add)
                    v.tensor_tensor(E.mix[:, :, :], E.one[:, 0, :, :], E.one[:, 1, :, :], ALU.add)
                    v.tensor_tensor(E.pick[:, :, :], E.one[:, 2, :, :], E.one[:, 3, :, :], ALU.add).then_inc(select, 1)
                    v.wait_ge(x_mm, q + 1)
                    for b in range(2):
                        v.tensor_tensor(E.xT[:, 4 * b:4 * b + 4, :], ps[:, 4 + b, :].rearrange("p (k n) -> p k n", k=4),
                                        mid(E.fng[:, 4 * b:4 * b + 4], P), ALU.mult).then_inc(x_out, 1)
                    v.wait_ge(gate_out, q + 1)
                    v.tensor_tensor(E.hid[:, :], E.act[:, :], ps[:, 1, :], ALU.mult).then_inc(hid, 1)
                    v.wait_ge(c_mm, q + 1)
                    for t in range(TT):
                        i = v.tensor_tensor(K.h[:, t, :], K.h[:, t, :], ps[:, 4 + 2 * t:6 + 2 * t, :].rearrange("p b n -> p (b n)"),
                                            ALU.add)
                    i.then_inc(vs, 1)
                    v.wait_ge(vs, q * 2 + 2)
                    v.sem_inc(summed, 1)


def stage_final_norm(K, M):
    nc, sem = K.nc, K.sem
    ld, root, done = sem("f_ld"), sem("f_root"), sem("f_done")
    with nc.Block() as block:

        @block.scalar
        def _(a):
            a.dma_start(M.fg[:, :], K.dram["final_norm"].partition_broadcast(P)).then_inc(ld, 16)
            for t in range(TT):
                K.ac(a, a.activation(M.junk[:, :], K.h[:, t, :], ACT.Square, accum_out=M.ss[:, t:t + 1]))
            a.activation(M.ss[:, :], M.ss[:, :], ACT.Sqrt, bias=K.eps[:, 0:1], scale=1.0 / D).then_inc(root, 1)

        @block.vector
        def _(v):
            v.wait_ge(root, 1)
            K.vc(v, v.reciprocal(M.ss[:, :], M.ss[:, :]))
            v.wait_ge(ld, 16)
            for t in range(TT):
                K.vc(v, v.tensor_scalar(K.h[:, t, :], K.h[:, t, :], M.ss[:, t:t + 1], None, ALU.mult))
                K.vc(v, v.tensor_tensor(K.h[:, t, :], K.h[:, t, :], M.fg[:, :], ALU.mult))


def norm_steps_vector(K, N, v, ready, ready_at, yscale, s, n):
    for t in range(TT):
        if t == 0:
            v.wait_ge(ready, ready_at)
        y = K.ps[:, 4 + 2 * t:6 + 2 * t, :].rearrange("p b n -> p (b n)")
        K.vc(v, v.scalar_tensor_tensor(out=K.h[:, t, :], in0=y, scalar=yscale, in1=N.ax[:, t, :], op0=ALU.mult, op1=ALU.add))
        v.bn_stats(N.stats[:, t, 0, :], K.h[:, t, 0:512])
        K.vc(v, v.bn_stats(N.stats[:, t, 1, :], K.h[:, t, 512:1024]))
        v.bn_aggr(N.mv[:, t, :], N.stats[:, t, :, :]).then_inc(s["mv"], 1)
    for t in range(TT):
        v.wait_ge(s["root"], TT * n + t + 1)
        K.vc(v, v.reciprocal(N.root[:, t:t + 1], N.root[:, t:t + 1]))
        K.vc(v, v.tensor_scalar(K.h[:, t, :], K.h[:, t, :], N.mv[:, t, 0:1], N.root[:, t:t + 1], ALU.subtract, ALU.mult))
        if t == 0:
            v.wait_ge(s["ld"], 32 * (n + 1))
        K.vc(v, v.tensor_tensor(K.h[:, t, :], K.h[:, t, :], N.g[:, :], ALU.mult))
        v.tensor_tensor(K.h[:, t, :], K.h[:, t, :], N.b[:, :], ALU.add).then_inc(s["x"], 1)


def norm_steps_scalar(K, N, a, s, n):
    for t in range(TT):
        a.wait_ge(s["mv"], TT * n + t + 1)
        a.activation(N.root[:, t:t + 1], N.mv[:, t, 1:2], ACT.Sqrt, bias=K.eps[:, 1:2]).then_inc(s["root"], 1)


def load_norm(K, N, a, s, layer, which):
    a.dma_start(N.g[:, :], K.dram["ln_g_2"][layer, which].partition_broadcast(P)).then_inc(s["ld"], 16)
    a.dma_start(N.b[:, :], K.dram["ln_b_2"][layer, which].partition_broadcast(P)).then_inc(s["ld"], 16)


def turn_x(K, pe, sem_turned):
    for t in range(TT):
        for k in range(KD):
            i = pe.transpose(K.ps[:, 2 * t + k // 4, (k % 4) * P:(k % 4 + 1) * P], K.h[:, t, k::KD], K.ident[:, :])
            if k % 4 == 3:
                i.then_inc(sem_turned, 1)


def stage_ffn(K, N, F, layer, which, n):
    nc, ps, sem, dram = K.nc, K.ps, K.sem, K.dram
    s, f = K.norm_sems, K.ffn_sems
    norms = K.norm_count
    K.norm_count += 1
    wg = dram["ffn_w_gate_2"][layer, which].rearrange("(p k) n -> p k n", k=KD)
    wu = dram["ffn_w_up_2"][layer, which].rearrange("(p k) n -> p k n", k=KD)
    wd = dram["ffn_w_down_2"][layer, which].rearrange("(f p) n -> p f n", p=P)
    base_t = 4 * K.turn_count
    K.turn_count += 1
    t0, g0 = 2 * NFC * n, NFC * n
    LOOPS = (NFC - 3) // 2
    before = [(NFC + 1) // 2 * n, NFC // 2 * n]

    with nc.Block() as block:

        @block.sync
        def _(sp):
            def load(c, b):
                col = slice(c * FC, (c + 1) * FC) if isinstance(c, int) else bass.ds(c * FC, FC)
                row = slice(c * 2, c * 2 + 2) if isinstance(c, int) else bass.ds(c * 2, 2)
                if not (isinstance(c, int) and c < 2):
                    sp.wait_ge(f["gu"], c * 2 + (t0 - 2))
                sp.dma_start(F.wg[:, b, :, :], wg[:, :, col]).then_inc(f["ld"][b], 16)
                sp.dma_start(F.wu[:, b, :, :], wu[:, :, col]).then_inc(f["ld"][b], 16)
                if not (isinstance(c, int) and c < 2):
                    sp.wait_ge(f["down"], c + (g0 - 1))
                sp.dma_start(F.wd[:, b, :, :], wd[:, row, :]).then_inc(f["ldd"][b], 16)
            load(0, 0)
            load(1, 1)
            with sp.Fori(0, LOOPS) as i:
                for b in range(2):
                    load(i * 2 + (2 + b), b)
            load(NFC - 1, (NFC - 1) % 2)

        @block.scalar
        def _(a):
            load_norm(K, N, a, s, layer, 2 * which)
            for t in range(TT):
                i = a.activation(N.ax[:, t, :], K.h[:, t, :], ACT.Copy, scale=ALPHA)
            i.then_inc(s["ax"], 1)

            def act(c, b):
                for j in range(2):
                    a.wait_ge(f["gu"], c * 2 + (t0 + j + 1))
                    if isinstance(c, int) and c < 2:
                        if n:
                            a.wait_ge(f["hid"], t0)
                    else:
                        a.wait_ge(f["hid"], c * 2 + (t0 + j - 3))
                    a.activation(F.act[:, b, j, :], ps[:, 2 * b + j, 0:S], ACT.Silu).then_inc(f["act"], 1)
            act(0, 0)
            act(1, 1)
            with a.Fori(0, LOOPS) as i:
                act(i * 2 + 2, 0)
                act(i * 2 + 3, 1)
            act(NFC - 1, 0)
            norm_steps_scalar(K, N, a, s, norms)

        @block.vector
        def _(v):
            for b in range(4):
                v.wait_ge(K.turned, base_t + b + 1)
                v.tensor_copy(N.xT[:, 4 * (b % 2):4 * (b % 2) + 4, (b // 2) * P:(b // 2 + 1) * P],
                              ps[:, b, :].rearrange("p (k n) -> p k n", k=4)).then_inc(K.xt_ready, 1)

            def hid(c, b):
                for j in range(2):
                    v.wait_ge(f["act"], c * 2 + (t0 + j + 1))
                    if not (isinstance(c, int) and c < 2):
                        v.wait_ge(f["down"], c + (g0 - 1))
                    v.tensor_tensor(F.hT[:, b, j, :], F.act[:, b, j, :], ps[:, 2 * b + j, S:2 * S], ALU.mult).then_inc(f["hid"], 1)
            hid(0, 0)
            hid(1, 1)
            with v.Fori(0, LOOPS) as i:
                hid(i * 2 + 2, 0)
                hid(i * 2 + 3, 1)
            hid(NFC - 1, 0)
            v.wait_ge(s["ax"], norms + 1)
            norm_steps_vector(K, N, v, f["down"], g0 + NFC, 0.5, s, norms)

        @block.tensor
        def _(pe):
            turn_x(K, pe, K.turned)
            pe.wait_ge(K.xt_ready, base_t + 4)

            def gate_up(c, b):
                if isinstance(c, int):
                    pe.wait_ge(f["ld"][b], 32 * (before[b] + c // 2 + 1))
                else:
                    pe.wait_ge(f["ld"][b], c * 16 + (32 * (before[b] + 1) - 16 * b))
                if not (isinstance(c, int) and c < 2):
                    pe.wait_ge(f["hid"], c * 2 + (t0 - 2))
                for j in range(2):
                    for w, o in ((F.wg, 0), (F.wu, S)):
                        for k in range(KD):
                            i = pe.matmul(ps[:, 2 * b + j, o:o + S], w[:, b, k, j * P:(j + 1) * P], N.xT[:, k, :],
                                          start=(k == 0), stop=(k == KD - 1))
                    i.then_inc(f["gu"], 1)

            def down(c, b, first=False, last=False):
                if isinstance(c, int):
                    pe.wait_ge(f["ldd"][b], 16 * (before[b] + c // 2 + 1))
                else:
                    pe.wait_ge(f["ldd"][b], c * 8 + (16 * (before[b] + 1) - 8 * b))
                pe.wait_ge(f["hid"], c * 2 + (t0 + 2))
                for j in range(2):
                    for t in range(TT):
                        for m in range(2):
                            i = pe.matmul(ps[:, 4 + 2 * t + m, :], F.hT[:, b, j, t * P:(t + 1) * P],
                                          F.wd[:, b, j, m * 512:(m + 1) * 512], start=(first and j == 0), stop=(last and j == 1))
                i.then_inc(f["down"], 1)

            gate_up(0, 0)
            gate_up(1, 1)
            down(0, 0, first=True)
            with pe.Fori(0, LOOPS) as i:
                gate_up(i * 2 + 2, 0)
                down(i * 2 + 1, 1)
                gate_up(i * 2 + 3, 1)
                down(i * 2 + 2, 0)
            gate_up(NFC - 1, 0)
            down(NFC - 2, 1)
            down(NFC - 1, 0, last=True)


def stage_memory(K, Y):
    nc, ps, sem = K.nc, K.ps, K.sem
    ld, ldw, turned, mt, mm, out = (sem("k_" + n) for n in ("ld", "ldw", "turned", "mt", "mm", "out"))
    with nc.Block() as block:

        @block.sync
        def _(sp):
            sp.dma_start(Y.mem[:, :, :], K.dram["mem_2"][0].rearrange("(t p) d -> p t d", p=P)).then_inc(ld, 16)
            for l in range(2):
                sp.dma_start(Y.wkv[:, l, :, :], K.dram["w_kv_mem_2"][l].rearrange("(p k) n -> p k n", k=KD)).then_inc(ldw, 16)

        @block.tensor
        def _(pe):
            pe.wait_ge(ld, 16)
            for t in range(TT):
                for k in range(KD):
                    i = pe.transpose(ps[:, 2 * t + k // 4, (k % 4) * P:(k % 4 + 1) * P], Y.mem[:, t, k::KD], K.ident[:, :])
            i.then_inc(turned, 1)
            pe.wait_ge(mt, 4)
            pe.wait_ge(ldw, 32)
            for l in range(2):
                for m in range(2):
                    for k in range(KD):
                        i = pe.matmul(ps[:, 4 * l + m, 0:NM], Y.wkv[:, l, k, m * P:(m + 1) * P], Y.memT[:, k, :],
                                      start=(k == 0), stop=(k == KD - 1))
                for t in range(TT):
                    for k in range(KD):
                        i = pe.matmul(ps[:, 4 * l + 2 + t, 0:XH * XD], Y.memT[:, k, t * P:(t + 1) * P], Y.wkv[:, l, k, 256:512],
                                      start=(k == 0), stop=(k == KD - 1))
                i.then_inc(mm, 1)

        @block.vector
        def _(v):
            v.wait_ge(turned, 1)
            for b in range(4):
                v.tensor_copy(Y.memT[:, 4 * (b % 2):4 * (b % 2) + 4, (b // 2) * P:(b // 2 + 1) * P],
                              ps[:, b, :].rearrange("p (k n) -> p k n", k=4)).then_inc(mt, 1)
            for l in range(2):
                v.wait_ge(mm, l + 1)
                for m in range(2):
                    v.tensor_copy(K.memk[:, l, 2 * m, :], ps[0:64, 4 * l + m, 0:NM])
                    v.tensor_copy(K.memk[:, l, 2 * m + 1, :], ps[64:128, 4 * l + m, 0:NM])
                v.tensor_copy(K.memv[:, l, :, :], ps[:, 4 * l + 2:4 * l + 4, 0:XH * XD])


def memory_attention(K, X, layer, s):
    ps = K.ps
    SC = XD ** -0.5

    def tensor(pe):
        pe.wait_ge(s["qx"], 2)
        for n in range(TT * XH):
            t, hh = divmod(n, XH)
            i = pe.matmul(ps[:, n // 2, (n % 2) * NM:(n % 2 + 1) * NM], X.qx[:, hh, t * P:(t + 1) * P], K.memk[:, layer, hh, :],
                          start=True, stop=True)
        i.then_inc(s["xs_mm"], 1)
        pe.wait_ge(s["xp"], TT * XH)
        for n in range(TT * XH):
            for m in range(2):
                i = pe.transpose(ps[:, n // 2, ((n % 2) * 2 + m) * P:((n % 2) * 2 + m + 1) * P],
                                 X.xp[:, n, m * P:(m + 1) * P], K.ident[:, :])
        i.then_inc(s["xt_mm"], 1)
        pe.wait_ge(s["xt_out"], 1)
        for n in range(TT * XH):
            t, hh = divmod(n, XH)
            for m in range(2):
                i = pe.matmul(ps[:, 4, n * XD:(n + 1) * XD], X.xpT[:, n, m, :], K.memv[:, layer, m, hh * XD:(hh + 1) * XD],
                              start=(m == 0), stop=(m == 1))
        i.then_inc(s["xo_mm"], 1)
        pe.wait_ge(s["xo_out"], 1)
        for m in range(2):
            for t in range(TT):
                i = pe.transpose(ps[:, 5, m * S + t * P:m * S + (t + 1) * P], X.xo[:, t, m * P:(m + 1) * P], K.ident[:, :])
        i.then_inc(s["xy_mm"], 1)

    def scalar(a):
        a.wait_ge(s["xmax"], 1)
        for n in range(TT * XH):
            a.activation(X.xp[:, n, :], ps[:, n // 2, (n % 2) * NM:(n % 2 + 1) * NM], ACT.Exp, bias=X.xmx[:, n:n + 1],
                         scale=SC, accum_out=X.xsum[:, n:n + 1]).then_inc(s["xp"], 1)
        a.wait_ge(s["xt_mm"], 1)
        a.activation(X.xpT[:, :, :, :].rearrange("p n m t -> p (n m t)"), ps[:, 0:4, :].rearrange("p b n -> p (b n)"),
                     ACT.Copy).then_inc(s["xt_out"], 1)

    def vector_max(v):
        v.wait_ge(s["xs_mm"], 1)
        K.vc(v, v.tensor_reduce(X.xmx[:, :], ps[:, 0:4, :].rearrange("p b (n m) -> p (b n) m", n=2), AX.X, ALU.max))
        v.tensor_scalar(X.xmx[:, :], X.xmx[:, :], -SC, None, ALU.mult).then_inc(s["xmax"], 1)

    def vector_out(v):
        v.wait_ge(s["xp"], TT * XH)
        K.vc(v, v.reciprocal(X.xsum[:, :], X.xsum[:, :]))
        v.wait_ge(s["xo_mm"], 1)
        v.tensor_tensor(X.xo[:, :, :].rearrange("p t (h e) -> p (t h) e", h=XH),
                        ps[:, 4, :].rearrange("p (n e) -> p n e", e=XD), mid(X.xsum[:, :], XD), ALU.mult).then_inc(s["xo_out"], 1)
        v.wait_ge(s["xy_mm"], 1)
        v.tensor_copy(X.mixT[:, 6:8, :], ps[:, 5, :].rearrange("p (m t) -> p m t", m=2)).then_inc(s["xy_out"], 1)

    return tensor, scalar, vector_max, vector_out


def out_project(K, X, pe, s):
    pe.wait_ge(s["ldo"], 16)
    for t in range(TT):
        for k in range(KD):
            for m in range(2):
                i = pe.matmul(K.ps[:, 4 + 2 * t + m, :], X.mixT[:, k, t * P:(t + 1) * P], X.wo[:, k, m * 512:(m + 1) * 512],
                              start=(k == 0), stop=(k == KD - 1))
    i.then_inc(s["out_mm"], 1)


MIX_SEMS = ("ldo", "ldc", "qx", "xs_mm", "xmax", "xp", "xt_mm", "xt_out", "xo_mm", "xo_out", "xy_mm", "xy_out", "out_mm",
            "z_mm", "z_out", "mix")


def stage_conv_mixer(K, N, X, layer, n_norm):
    nc, ps, sem, dram = K.nc, K.ps, K.sem, K.dram
    s = {n: sem("c_" + n) for n in MIX_SEMS + ("c_gate",)}
    ns, norms = K.norm_sems, K.norm_count
    K.norm_count += 1
    base_t = 4 * K.turn_count
    K.turn_count += 1
    w = dram["w_in_conv_2"][0].rearrange("(p k) n -> p k n", k=KD)
    NCK = 10
    order = [3, 6, 4, 7, 5, 8, 0, 1, 2, 9]
    R = len(order)
    lds = [sem(f"c_ld{n}") for n in range(4)]
    xa_pe, xa_act, xa_max, xa_out = memory_attention(K, X, layer, s)
    NT = 6
    bank = lambda n: n % 8

    with nc.Block() as block:

        @block.sync
        def _(sp):
            for n, c in enumerate(order):
                sp.dma_start(X.w[:, n, :, 0:FC], w[:, :, c * FC:(c + 1) * FC]).then_inc(X.ldw[n], 16)
            sp.dma_start(X.wo[:, :, :], dram["w_out_2"][layer].rearrange("(k p) n -> p k n", p=P)).then_inc(s["ldo"], 16)

        @block.tensor
        def _(pe):
            turn_x(K, pe, K.turned)
            pe.wait_ge(K.xt_ready, base_t + 4)
            for n in range(R):
                pe.wait_ge(X.ldw[n], 16)
                if n >= 8:
                    pe.wait_ge(s["z_out"], n - 7)
                for j in range(2):
                    for k in range(KD):
                        i = pe.matmul(ps[:, bank(n), j * S:(j + 1) * S], X.w[:, n, k, j * P:(j + 1) * P], N.xT[:, k, :],
                                      start=(k == 0), stop=(k == KD - 1))
                i.then_inc(s["z_mm"], 1)
            pe.wait_ge(s["z_out"], R)
            xa_pe(pe)
            pe.wait_ge(s["xy_out"], 1)
            out_project(K, X, pe, s)

        @block.scalar
        def _(a):
            load_norm(K, N, a, ns, layer, 1)
            for j in range(CW):
                a.dma_start(X.cw[:, :, j], dram["conv_w_2"][0, j].rearrange("(i p) -> p i", p=P),
                            allow_slow_non_contiguous=True).then_inc(s["ldc"], 16)
            for t in range(TT):
                i = a.activation(N.ax[:, t, :], K.h[:, t, :], ACT.Copy, scale=ALPHA)
            i.then_inc(ns["ax"], 1)
            for g in range(3):
                a.wait_ge(s["z_mm"], 2 * g + 1)
                a.activation(X.cg[:, 2 * g:2 * g + 2, :], ps[:, bank(2 * g), :].rearrange("p (j t) -> p j t", j=2),
                             ACT.Copy).then_inc(s["c_gate"], 1)
            xa_act(a)
            norm_steps_scalar(K, N, a, ns, norms)

        @block.vector
        def _(v):
            K.vc(v, v.memset(X.pad[:, 0:NT, 0:CW - 1], 0.0))
            for b in range(4):
                v.wait_ge(K.turned, base_t + b + 1)
                v.tensor_copy(N.xT[:, 4 * (b % 2):4 * (b % 2) + 4, (b // 2) * P:(b // 2 + 1) * P],
                              ps[:, b, :].rearrange("p (k n) -> p k n", k=4)).then_inc(K.xt_ready, 1)
            v.wait_ge(s["ldc"], 16 * CW)
            E = CW - 1
            for g in range(3):
                v.wait_ge(s["c_gate"], g + 1)
                v.wait_ge(s["z_mm"], 2 * g + 2)
                i = v.tensor_tensor(X.pad[:, 2 * g:2 * g + 2, E:E + S], X.cg[:, 2 * g:2 * g + 2, :],
                                    ps[:, bank(2 * g + 1), :].rearrange("p (j t) -> p j t", j=2), ALU.mult)
                i.then_inc(s["z_out"], 2)
                v.wait_ge(s["z_out"], 2 * g + 2)
                for j in range(2):
                    m = 2 * g + j
                    K.vc(v, v.tensor_scalar(X.cv[:, m, :], X.pad[:, m, E:E + S], X.cw[:, m, CW - 1:CW], None, ALU.mult))
                    for q in range(CW - 1):
                        K.vc(v, v.scalar_tensor_tensor(out=X.cv[:, m, :], in0=X.pad[:, m, q:q + S], scalar=X.cw[:, m, q:q + 1],
                                                       in1=X.cv[:, m, :], op0=ALU.mult, op1=ALU.add))
            for g in range(3):
                v.wait_ge(s["z_mm"], 7 + g)
                v.tensor_tensor(X.mixT[:, 2 * g:2 * g + 2, :], X.cv[:, 2 * g:2 * g + 2, :],
                                ps[:, bank(6 + g), :].rearrange("p (j t) -> p j t", j=2), ALU.mult).then_inc(s["z_out"], 1)
            v.wait_ge(s["z_mm"], R)
            q = ps[:, bank(R - 1), :].rearrange("p (j t) -> p j t", j=2)
            v.tensor_copy(X.qx[:, 0::2, :], q[0:64, :, :]).then_inc(s["qx"], 1)
            v.wait_ge(s["qx"], 1)
            v.tensor_copy(X.qx[:, 1::2, :], q[64:128, :, :]).then_inc(s["qx"], 1)
            v.wait_ge(s["qx"], 2)
            v.sem_inc(s["z_out"], 1)
            xa_max(v)
            xa_out(v)
            v.wait_ge(ns["ax"], norms + 1)
            norm_steps_vector(K, N, v, s["out_mm"], 1, 1.0, ns, norms)


def stage_mlstm_mixer(K, N, X, layer, n_norm):
    nc, ps, sem, dram = K.nc, K.ps, K.sem, K.dram
    s = {n: sem("l_" + n) for n in MIX_SEMS + ("na", "lf", "em_in", "em", "row", "bc_mm", "col_mm", "col", "wt", "masked",
                                               "qk_ready", "sc_mm", "pt", "num_mm", "hv", "hroot", "silu", "y", "y_mm", "y_out",
                                               "opre")}
    ns, norms = K.norm_sems, K.norm_count
    K.norm_count += 1
    base_t = 4 * K.turn_count
    K.turn_count += 1
    w = dram["w_in_mlstm_2"][0].rearrange("(p k) n -> p k n", k=KD)
    GQ = 2 * HH + XH * XD
    cols = [(4 * TOK, GQ)] + [(n * FC, FC) for n in range(12)]
    R = X.w.shape[1]
    xa_pe, xa_act, xa_max, xa_out = memory_attention(K, X, layer, s)
    NT = 12
    E = QW - 1
    bank = lambda n: n % 8
    PART = [(0, 1, 0), (2, 1, 64), (3, 4, 0), (5, 4, 64)]

    with nc.Block() as block:

        @block.sync
        def _(sp):
            for n, (c, m) in enumerate(cols):
                if n >= R:
                    sp.wait_ge(s["z_mm"], n - R + 1)
                base = X.ldw_used[n % R]
                X.ldw_used[n % R] += 16
                X.ldw_at[n] = base + 16
                sp.dma_start(X.w[:, n % R, :, 0:m], w[:, :, c:c + m]).then_inc(X.ldw[n % R], 16)
            sp.dma_start(X.wo[:, :, :], dram["w_out_2"][layer].rearrange("(k p) n -> p k n", p=P)).then_inc(s["ldo"], 16)

        @block.tensor
        def _(pe):
            turn_x(K, pe, K.turned)
            pe.wait_ge(K.xt_ready, base_t + 4)
            for n, (c, m) in enumerate(cols):
                pe.wait_ge(X.ldw[n % R], X.ldw_at[n])
                if n >= 8:
                    pe.wait_ge(s["z_out"], n - 7)
                W = X.w[:, n % R, :, :]
                if n == 0:
                    pe.wait_ge(K.xt_ready, base_t + 4)
                    for j in range(2):
                        for k in range(KD):
                            pe.matmul(ps[0:HH, 0, j * S:(j + 1) * S], W[:, k, j * HH:(j + 1) * HH], N.xT[:, k, :],
                                      start=(k == 0), stop=(k == KD - 1))
                    for j in range(2):
                        for k in range(KD):
                            i = pe.matmul(ps[:, 7, j * S:(j + 1) * S], W[:, k, 2 * HH + j * P:2 * HH + (j + 1) * P], N.xT[:, k, :],
                                          start=(k == 0), stop=(k == KD - 1))
                elif n <= 6:
                    for j in range(2):
                        for k in range(KD):
                            i = pe.matmul(ps[:, bank(n), j * S:(j + 1) * S], W[:, k, j * P:(j + 1) * P], N.xT[:, k, :],
                                          start=(k == 0), stop=(k == KD - 1))
                else:
                    if n == 7:
                        pe.wait_ge(s["qx"], 2)
                    for t in range(TT):
                        for k in range(KD):
                            i = pe.matmul(ps[:, bank(n), t * FC:(t + 1) * FC], N.xT[:, k, t * P:(t + 1) * P], W[:, k, 0:FC],
                                          start=(k == 0), stop=(k == KD - 1))
                i.then_inc(s["z_mm"], 1)
            pe.wait_ge(s["z_out"], len(cols))
            xa_pe(pe)
            pe.wait_ge(s["xy_out"], 1)
            pe.wait_ge(s["row"], 1)
            pe.wait_ge(s["em"], 1)
            for hh in range(HH):
                i = pe.matmul(ps[:, hh // 2, (hh % 2) * S:(hh % 2 + 1) * S], X.rowsel[:, hh, :], X.Mr[:, :], start=True, stop=True)
            i.then_inc(s["bc_mm"], 1)
            for t in range(TT):
                pe.transpose(ps[:, 2, t * HH:(t + 1) * HH], X.ar[:, t * P:(t + 1) * P], K.ident[0:HH, 0:HH])
                i = pe.transpose(ps[:, 2, 8 + t * HH:8 + (t + 1) * HH], X.em[:, t * P:(t + 1) * P], K.ident[0:HH, 0:HH])
            i.then_inc(s["col_mm"], 1)
            pe.wait_ge(s["qk_ready"], 1)
            for st in range(TT):
                for hh in range(HH):
                    o = ps[:, 4 + st * 2 + hh // 2, (hh % 2) * S:(hh % 2 + 1) * S]
                    A, B, lo = PART[hh]
                    pe.matmul(o, X.qk[:, 6 + A, st * P:(st + 1) * P], X.qk[:, A, :], start=True, stop=False)
                    kb = X.qk[0:64, 6 + B, :] if lo == 0 else X.qkh[:, 2 + hh // 2, :]
                    qb = X.qk[0:64, B, :] if lo == 0 else X.qkh[:, hh // 2, :]
                    i = pe.matmul(o, kb[:, st * P:(st + 1) * P], qb, start=False, stop=True)
            i.then_inc(s["sc_mm"], 1)
            pe.wait_ge(s["pt"], 4)
            pe.wait_ge(s["col"], 1)
            for t in range(TT):
                for hh in range(HH):
                    o = ps[:, 2 * t + hh // 2, (hh % 2) * 256:(hh % 2) * 256 + HD + 1]
                    for st in range(t + 1):
                        i = pe.matmul(o, X.wt[:, st, hh, t * P:(t + 1) * P], X.va[:, st, hh, :], start=(st == 0), stop=(st == t))
            i.then_inc(s["num_mm"], 1)
            pe.wait_ge(s["y"], 1)
            for m in range(6):
                for t in range(TT):
                    i = pe.transpose(ps[:, m // 2, (m % 2) * S + t * P:(m % 2) * S + (t + 1) * P], X.hh[:, t, m * P:(m + 1) * P],
                                     K.ident[:, :])
            i.then_inc(s["y_mm"], 1)
            pe.wait_ge(s["y_out"], 1)
            out_project(K, X, pe, s)

        @block.scalar
        def _(a):
            load_norm(K, N, a, ns, layer, 1)
            for j in range(QW):
                a.dma_start(X.qw[:, :, j], dram["qk_conv_w_2"][0, j].rearrange("(i p) -> p i", p=P),
                            allow_slow_non_contiguous=True).then_inc(s["ldc"], 16)
            a.dma_start(X.bg[:, :], dram["b_gates_2"][0].rearrange("(j h) -> h j", h=HH), allow_slow_non_contiguous=True).then_inc(s["ldc"], 16)
            a.dma_start(X.hg[:, :], dram["head_norm_g_2"][0].rearrange("h d -> (h d)").partition_broadcast(P)).then_inc(s["ldc"], 16)
            for t in range(TT):
                i = a.activation(N.ax[:, t, :], K.h[:, t, :], ACT.Copy, scale=ALPHA)
            i.then_inc(ns["ax"], 1)
            a.wait_ge(s["na"], 1)
            K.ac(a, a.activation(X.fe[:, :], X.fe[:, :], ACT.Exp))
            a.activation(X.fe[:, :], X.fe[:, :], ACT.Ln, bias=K.eps[0:HH, 2:3]).then_inc(s["lf"], 1)
            a.wait_ge(s["em_in"], 1)
            a.activation(X.em[:, :], X.em[:, :], ACT.Exp, scale=-1.0).then_inc(s["em"], 1)
            a.wait_ge(s["mix"], 1)
            a.activation(X.qk[:, :, :], X.cv[:, :, :], ACT.Silu).then_inc(s["silu"], 1)
            xa_act(a)
            a.wait_ge(s["bc_mm"], 1)
            a.wait_ge(s["col"], 1)
            for st in range(TT):
                for hh in range(HH):
                    a.activation(X.wt[:, st, hh, :], ps[:, hh // 2, (hh % 2) * S:(hh % 2 + 1) * S], ACT.Exp,
                                 bias=X.col[:, st * HH + hh:st * HH + hh + 1], scale=-1.0).then_inc(s["wt"], 1)
            a.wait_ge(s["z_out"], len(cols))
            a.activation(X.og[:, :, :], X.og[:, :, :], ACT.Sigmoid).then_inc(s["opre"], 1)
            a.wait_ge(s["hv"], 1)
            a.activation(X.hrs[:, :], X.hmv[:, :, 1], ACT.Sqrt, bias=K.eps[:, 1:2]).then_inc(s["hroot"], 1)
            norm_steps_scalar(K, N, a, ns, norms)

        @block.gpsimd
        def _(g):
            g.wait_ge(s["wt"], TT * HH)
            g.affine_select(out=X.wt[:, 0, :, :], in_=X.wt[:, 0, :, :], compare_op=ALU.is_ge, fill=0.0, base=0,
                            pattern=[[0, HH], [1, S]], channel_multiplier=-1).then_inc(s["masked"], 1)
            g.affine_select(out=X.wt[:, 1, :, :], in_=X.wt[:, 1, :, :], compare_op=ALU.is_ge, fill=0.0, base=-P,
                            pattern=[[0, HH], [1, S]], channel_multiplier=-1).then_inc(s["masked"], 1)

        @block.vector
        def _(v):
            c = lambda i: K.vc(v, i)
            for hh in range(HH):
                c(v.tensor_copy(X.rowsel[:, hh, :], K.ident[0:HH, hh:hh + 1].broadcast_to([HH, P])))
            c(v.memset(X.pad[:, :, 0:E], 0.0))
            c(v.memset(X.va[:, :, :, HD:HD + 1], 1.0))
            for b in range(4):
                v.wait_ge(K.turned, base_t + b + 1)
                v.tensor_copy(N.xT[:, 4 * (b % 2):4 * (b % 2) + 4, (b // 2) * P:(b // 2 + 1) * P],
                              ps[:, b, :].rearrange("p (k n) -> p k n", k=4)).then_inc(K.xt_ready, 1)
            v.wait_ge(s["ldc"], 16 * (QW + 2))
            v.wait_ge(s["z_mm"], 1)
            c(v.tensor_scalar(X.ar[:, :], ps[0:HH, 0, 0:S], X.bg[:, 0:1], None, ALU.add))
            c(v.tensor_scalar(X.fx[:, :], ps[0:HH, 0, S:2 * S], X.bg[:, 1:2], None, ALU.add))
            v.sem_inc(s["z_out"], 1)
            q = ps[:, 7, :].rearrange("p (j t) -> p j t", j=2)
            v.tensor_copy(X.qx[:, 0::2, :], q[0:64, :, :]).then_inc(s["qx"], 1)
            v.tensor_copy(X.qx[:, 1::2, :], q[64:128, :, :]).then_inc(s["qx"], 1)
            v.scalar_tensor_tensor(out=X.fe[:, :], in0=X.fx[:, :], scalar=-1.0, in1=X.fx[:, :], op0=ALU.mult,
                                   op1=ALU.min).then_inc(s["na"], 1)
            v.wait_ge(s["lf"], 1)
            c(v.scalar_tensor_tensor(out=X.fx[:, :], in0=X.fx[:, :], scalar=0.0, in1=X.fe[:, :], op0=ALU.min, op1=ALU.subtract))
            c(v.tensor_tensor_scan(X.fe[:, :], K.ones4[:, :], X.fx[:, :], 0.0, ALU.mult, ALU.add))
            c(v.tensor_tensor(X.ar[:, :], X.ar[:, :], X.fe[:, :], ALU.subtract))
            c(v.tensor_tensor_scan(X.Mr[:, :], X.ar[:, :], X.ar[:, :], 0.0, ALU.max, ALU.max))
            v.sem_inc(s["row"], 1)
            v.tensor_tensor(X.em[:, :], X.fe[:, :], X.Mr[:, :], ALU.add).then_inc(s["em_in"], 1)
            for n in range(1, 7):
                v.wait_ge(s["z_mm"], n + 1)
                v.tensor_copy(X.pad[:, 2 * n - 2:2 * n, E:E + S], ps[:, bank(n), :].rearrange("p (j t) -> p j t", j=2))\
                 .then_inc(s["z_out"], 1)
                v.wait_ge(s["z_out"], n + 1)
                for m in (2 * n - 2, 2 * n - 1):
                    c(v.tensor_scalar(X.cv[:, m, :], X.pad[:, m, E:E + S], X.qw[:, m, QW - 1:QW], None, ALU.mult))
                    for j in range(QW - 1):
                        c(v.scalar_tensor_tensor(out=X.cv[:, m, :], in0=X.pad[:, m, j:j + S], scalar=X.qw[:, m, j:j + 1],
                                                 in1=X.cv[:, m, :], op0=ALU.mult, op1=ALU.add))
            v.sem_inc(s["mix"], 1)
            for n in range(7, 10):
                v.wait_ge(s["z_mm"], n + 1)
                for t in range(TT):
                    lo = (n - 7) * FC
                    while lo < (n - 6) * FC:
                        hh, off = divmod(lo, HD)
                        m = min(HD - off, (n - 6) * FC - lo)
                        f = lo - (n - 7) * FC
                        c(v.tensor_copy(X.va[:, t, hh, off:off + m], ps[:, bank(n), t * FC + f:t * FC + f + m]))
                        lo += m
                v.sem_inc(s["z_out"], 1)
            for n in range(10, 13):
                v.wait_ge(s["z_mm"], n + 1)
                v.tensor_copy(X.og[:, :, (n - 10) * FC:(n - 9) * FC], ps[:, bank(n), :].rearrange("p (t f) -> p t f", t=TT))\
                 .then_inc(s["z_out"], 1)
            v.wait_ge(s["silu"], 1)
            c(v.tensor_copy(X.qkh[:, 0, :], X.qk[64:128, 1, :]))
            c(v.tensor_copy(X.qkh[:, 1, :], X.qk[64:128, 4, :]))
            c(v.tensor_copy(X.qkh[:, 2, :], X.qk[64:128, 7, :]))
            c(v.tensor_copy(X.qkh[:, 3, :], X.qk[64:128, 10, :]))
            v.sem_inc(s["qk_ready"], 1)
            xa_max(v)
            xa_out(v)
            v.wait_ge(s["col_mm"], 1)
            v.tensor_copy(X.col[:, :], ps[:, 2, 0:16]).then_inc(s["col"], 1)
            v.wait_ge(s["sc_mm"], 1)
            for st in range(TT):
                v.wait_ge(s["masked"], st + 1)
                for g in range(2):
                    v.scalar_tensor_tensor(out=X.wt[:, st, 2 * g:2 * g + 2, :].rearrange("p h t -> p (h t)"), in0=ps[:, 4 + 2 * st + g, :],
                                           scalar=HD ** -0.5, in1=X.wt[:, st, 2 * g:2 * g + 2, :].rearrange("p h t -> p (h t)"),
                                           op0=ALU.mult, op1=ALU.mult).then_inc(s["pt"], 1)
            v.wait_ge(s["num_mm"], 1)
            num = ps[:, 0:4, :].rearrange("p b (j n) -> p (b j) n", j=2)
            c(v.tensor_copy(X.den[:, :, :], num[:, :, HD:HD + 1]))
            den = X.den[:, :, 0]
            c(v.scalar_tensor_tensor(out=den, in0=den, scalar=-1.0, in1=den, op0=ALU.mult, op1=ALU.max))
            c(v.tensor_tensor(den, den, X.col[:, 8:16], ALU.max))
            c(v.reciprocal(den, den))
            hv = X.hh[:, :, :].rearrange("p t (h e) -> p (t h) e", h=HH)
            c(v.tensor_tensor(hv, num[:, :, 0:HD], mid(den, HD), ALU.mult))
            for n in range(TT * HH - 1):
                v.bn_stats(X.hst[:, n, :], hv[:, n, :])
            c(v.bn_stats(X.hst[:, 7, :], hv[:, 7, :]))
            for n in range(TT * HH):
                i = v.bn_aggr(X.hmv[:, n, :], X.hst[:, n, :])
            i.then_inc(s["hv"], 1)
            v.wait_ge(s["hroot"], 1)
            c(v.reciprocal(X.hrs[:, :], X.hrs[:, :]))
            for n in range(TT * HH):
                i = v.tensor_scalar(hv[:, n, :], hv[:, n, :], X.hmv[:, n, 0:1], X.hrs[:, n:n + 1], ALU.subtract, ALU.mult)
            c(i)
            c(v.tensor_tensor(X.hh[:, :, :], X.hh[:, :, :], rep(X.hg[:, :], TT), ALU.mult))
            v.wait_ge(s["opre"], 1)
            v.tensor_tensor(X.hh[:, :, :], X.hh[:, :, :], X.og[:, :, :], ALU.mult).then_inc(s["y"], 1)
            v.wait_ge(s["y_mm"], 1)
            v.tensor_copy(X.mixT[:, 0:6, :], ps[:, 0:3, :].rearrange("p b (m t) -> p (b m) t", m=2)).then_inc(s["y_out"], 1)
            v.wait_ge(ns["ax"], norms + 1)
            norm_steps_vector(K, N, v, s["out_mm"], 1, 1.0, ns, norms)


def tiles(nc, ctx, into, prefix, **shapes):
    for name, (shape, dt) in shapes.items():
        into.tiles[name] = ctx.enter_context(nc.sbuf_tensor(prefix + name, list(shape), dt))
    return into


def f(*shape):
    return (shape, F32)


class StageSemaphores:

    def __init__(self, K):
        self.K, self.ctx, self.got = K, ExitStack(), []

    def __enter__(self):
        self.outer = self.K.sem
        self.K.sem = self.take
        return self

    def take(self, name):
        self.got.append(self.ctx.enter_context(self.K.nc.semaphore(name)))
        return self.got[-1]

    def __exit__(self, *_):
        self.K.sem = self.outer
        nums = sorted(x.num for x in self.got)
        runs = []
        for n in nums:
            if runs and runs[-1].stop == n:
                runs[-1] = range(runs[-1].start, n + 1)
            else:
                runs.append(range(n, n + 1))
        with self.K.nc.Block() as block:

            @block.sync
            def _(sp):
                for r in runs:
                    sp.sem_clear(r)
        self.ctx.close()


def network(nc, dram, out, stop=None, debug=None):
    K = Kit()
    K.nc, K.dram = nc, dram
    K.norm_count = K.turn_count = 0
    with ExitStack() as ctx:
        K.sem = lambda name: ctx.enter_context(nc.semaphore(name))
        K.vc, K.ac, K.pc = Chain(K.sem("v_chain")), Chain(K.sem("a_chain")), Chain(K.sem("p_chain"))
        K.norm_sems = {n: K.sem("n_" + n) for n in ("ld", "mv", "root", "x", "ax")}
        K.ffn_sems = {n: K.sem("w_" + n) for n in ("gu", "act", "hid", "down")}
        K.ffn_sems["ld"] = [K.sem("w_ld0"), K.sem("w_ld1")]
        K.ffn_sems["ldd"] = [K.sem("w_ldd0"), K.sem("w_ldd1")]
        K.turned, K.xt_ready = K.sem("x_turned"), K.sem("xt_ready")
        K.ps = ctx.enter_context(nc.psum_tensor("banks", [P, 8, 512], F32))
        tiles(nc, ctx, K, "c_", ident=f(P, P), ones=f(P, P), earlier=f(P, P), iota=f(P, P), iota_i=((P, P), I32), eps=f(P, 4),
              h=f(P, TT, D), ones4=f(HH, S), memk=f(64, 2, XH, NM), memv=f(P, 2, TT, XH * XD))
        out_sem = K.sem("out_stored")

        def finish(pairs):
            with nc.Block() as block:
                @block.sync
                def _(sp):
                    for n, (dst, src) in enumerate(pairs):
                        sp.dma_start(dst, src).then_inc(out_sem, 16)
                    sp.wait_ge(out_sem, 16 * len(pairs))

        stage_constants(K)
        with ExitStack() as moe_ctx:
            tiles(nc, moe_ctx, K, "k_", u=f(P, TT, D), gate=f(P, 2, TT), slot=f(P, 2, TT), table=((1, QUADS * QUAD + 1), I32))
            E = tiles(nc, moe_ctx, Kit(), "e_", fng=f(P, KD))
            with ExitStack() as c1:
                M = Kit()
                M.ld_small, M.n_small, M.ld_wout = K.sem("ld_small"), 14, K.sem("ld_wout")
                M.fng = E.fng
                tiles(nc, c1, M, "m_", uT=f(P, KD, L), yT=f(P, KD, S), wout=f(P, KD, D), wr=f(P, KD, NG + NE), br=f(P, NG + NE),
                      junk=f(P, D), ss=f(P, 2), rs=f(P, 2))
                with ExitStack() as c2:
                    tiles(nc, c2, M, "m_", mixg=f(P, KD), wa2=f(RANK, GH * DK), ba=f(DK, GH), gg=f(CH, GH * DV), qg=f(P, 2),
                          kvg=f(P, 1), wqb=f(P, 2, 768), wkvb=f(P, 1024), cos=f(ROPE, L), sin=f(ROPE, L),
                          qT=f(DK, GH, L), kT=f(DK, GH, L), krT=f(ROPE, L), alT=f(RANK, L), lat=f(P, TT, QR + KVR),
                          latM=f(META, KVR), v=f(CH, NCH + 1, GH * DV), r=f(CH, NCH, GH * DV))
                    with ExitStack() as c3:
                        tiles(nc, c3, M, "m_", hM=f(META, D), uM=f(META, D), ssM=f(META, 1), rsM=f(META, 1), Wi=f(P, KD, D_IN))
                        stage_project(K, M)
                    with ExitStack() as c3, StageSemaphores(K):
                        tiles(nc, c3, M, "m_", gx=f(DK, GH, L), ge=f(DK, GH, L), gl=f(DK, GH, L), gb=f(DK, GH, L),
                              keep=f(DK, GH, L), eb=f(DK, GH, L), enb=f(DK, GH, L), ekb=f(DK, GH, L), dec=f(DK, GH, NCH + 1),
                              qe=f(DK, GH, S), ke=f(DK, GH, S), kw=f(DK, GH, L), att=f(CH, NCH * GH, CH), kwc=f(CH, NCH * GH, DK),
                              st=f(DK, NCH, GH, DV), o=f(CH, NCH, GH * DV), oss=f(CH, NCH * GH))
                        M.osq = M.uT[0:CH, :, :].rearrange("p k n -> p (k n)")[:, 0:NCH * GH * DV].rearrange("p (n e) -> p n e", e=DV)
                        stage_gla(K, M)
                    with ExitStack() as c3, StageSemaphores(K):
                        tiles(nc, c3, M, "m_", lss=f(P, 4), lssM=f(META, 1), qlT=f(P, 2, S), kvT=f(P, L), kn=f(P, MH, L),
                              qn=f(P, MH, S), vv=f(P, TT, MH * MV), vvM=f(META, MH * MV), sc=f(P, TT * MH, L), mx=f(P, TT * MH),
                              rsum=f(P, TT * MH), kr=f(ROPE, L), qr=f(ROPE, MH, S), rt=f(ROPE, MH, L), pt=f(P, 12, P),
                              ptM=f(META, TT * MH, P), ym=f(P, TT, MH * MV))
                        stage_mla(K, M)
                if stop == "mix":
                    return finish([(debug["yT"], M.yT[:, :, :])])
                with ExitStack() as c2, StageSemaphores(K):
                    tiles(nc, c2, M, "r_", lg=f(P, TT, NG + NE), t0=f(P, TT), t1=f(P, TT), ge8=f(P, TT, NG), tmp8=f(P, TT, EG),
                          gh=f(P, TT, NG), gp=f(P, TT), e64=f(P, TT, NE), sel=f(P, TT, EG), m1=f(P, TT), m2=f(P, TT),
                          h1=f(P, TT, EG), h2=f(P, TT, EG), ee=f(P, TT), x1=f(P, TT, NE), x2=f(P, TT, NE), hot=f(P, TT, NE),
                          cnt=f(P, NE), gtm=f(P, NE, RANKS), nb=f(P, NE), ends=f(P, NE), ecol=f(NE, 1), cmp=f(NE, QUADS * QUAD),
                          pos=f(P, TT, NE), i8=f(P, TT, EG), i8i=((P, TT, EG), I32), i32=f(P, NE, RANKS), i32i=((P, NE, RANKS), I32))
                    stage_route(K, M)
            if stop == "route":
                return finish([(debug["u"], K.u[:, :, :]), (debug["slot"], K.slot[:, :, :]), (debug["gate"], K.gate[:, :, :]),
                               (debug["table"], K.table[:, :])])
            tiles(nc, moe_ctx, E, "e_", W=f(P, 3, QUAD, 4 * DE), xT=f(P, KD, P), pick=f(P, TT, P), mix=f(P, TT, P), mixT=f(P, TT, P),
                  one=f(P, 4, TT, P), act=f(P, DE), hid=f(P, DE), hT=f(P, 4, P), y=f(P, D))
            stage_experts(K, E)
        with ExitStack() as c1:
            M = tiles(nc, c1, Kit(), "f_", fg=f(P, D), junk=f(P, D), ss=f(P, TT))
            stage_final_norm(K, M)
        with ExitStack() as c1:
            Y = tiles(nc, c1, Kit(), "y_", mem=f(P, TT, D), memT=f(P, KD, NM), wkv=f(P, 2, KD, 512))
            stage_memory(K, Y)
        if stop == "first":
            return finish([(debug["x"], K.h[:, :, :])])
        N = tiles(nc, ctx, Kit(), "n_", xT=f(P, KD, S), ax=f(P, TT, D), g=f(P, D), b=f(P, D), stats=f(P, TT, 2, 6), mv=f(P, TT, 2),
                  root=f(P, TT))
        ldw = [K.sem(f"ld_cols{n}") for n in range(10)]
        n = 0
        for layer in range(2):
            for part in range(3):
                with ExitStack() as c1:
                    if part != 1:
                        F = tiles(nc, c1, Kit(), f"w{n}_", wg=f(P, 2, KD, FC), wu=f(P, 2, KD, FC), wd=f(P, 2, 2, D),
                                  act=f(P, 2, 2, S), hT=f(P, 2, 2, S))
                        stage_ffn(K, N, F, layer, part // 2, n)
                        n += 1
                        if stop == f"x{layer}{part}":
                            return finish([(debug["x"], K.h[:, :, :])])
                        continue
                    X = tiles(nc, c1, Kit(), f"x{layer}_", wo=f(P, KD, D), mixT=f(P, KD, S), qx=f(XD, XH, S),
                              xp=f(P, TT * XH, NM), xpT=f(P, TT * XH, 2, P), xmx=f(P, TT * XH), xsum=f(P, TT * XH),
                              xo=f(P, TT, XH * XD))
                    X.ldw = ldw
                    c1.enter_context(StageSemaphores(K))
                    if layer == 0:
                        tiles(nc, c1, X, "x0_", w=f(P, 10, KD, FC), cw=f(P, 6, CW), cv=f(P, 6, S),
                              pad=f(P, 6, S + CW - 1))
                        X.cg = X.xp[:, 0:6, :]
                        stage_conv_mixer(K, N, X, layer, 0)
                    else:
                        X.ldw_used, X.ldw_at = [16] * 10, {}
                        tiles(nc, c1, X, "x1_", w=f(P, 3, KD, 264), qw=f(P, 12, QW), bg=f(HH, 2), hg=f(P, TOK),
                              pad=f(P, 12, S + QW - 1), cv=f(P, 12, S), qk=f(P, 12, S), qkh=f(64, 4, S), fx=f(HH, S), fe=f(HH, S),
                              ar=f(HH, S), Mr=f(HH, S), em=f(HH, S), rowsel=f(HH, HH, P), col=f(P, 16), wt=f(P, TT, HH, S),
                              va=f(P, TT, HH, HD + 1), og=f(P, TT, TOK), den=f(P, TT * HH, 1), hst=f(P, 8, 6),
                              hmv=f(P, 8, 2), hrs=f(P, 8))
                        X.hh = X.pad[:, :, :].rearrange("p i t -> p (i t)")[:, 0:TT * TOK].rearrange("p (t n) -> p t n", t=TT)
                        stage_mlstm_mixer(K, N, X, layer, 0)
                if stop == f"x{layer}{part}":
                    return finish([(debug["x"], K.h[:, :, :])])
        finish([(out.rearrange("(t p) d -> p t d", p=P), K.h[:, :, :])])


_INS = ['x', 'meta_tokens', 'mix_norm', 'w_in', 'gla_w_a2', 'gla_b_a', 'gla_out_norm', 'mla_q_norm', 'mla_w_qb',
        'mla_kv_norm', 'mla_w_kvb', 'w_out', 'ffn_norm', 'router_group_w', 'router_group_b', 'router_expert_w',
        'router_expert_b', 'expert_w_gate', 'expert_w_up', 'expert_w_down', 'final_norm', 'mem_2', 'ln_g_2', 'ln_b_2',
        'ffn_w_gate_2', 'ffn_w_up_2', 'ffn_w_down_2', 'w_kv_mem_2', 'w_out_2', 'w_in_conv_2', 'conv_w_2', 'w_in_mlstm_2',
        'b_gates_2', 'qk_conv_w_2', 'head_norm_g_2']


def rotary_tables():
    pos = np.concatenate([META + np.arange(S), np.arange(META)]).astype(np.float32)
    inv = (10000.0 ** (-np.arange(0, ROPE, 2) / ROPE)).astype(np.float32)
    ang = (inv[:, None] * pos[None, :]).astype(np.float32).astype(np.float64)
    c, s = np.cos(ang).astype(np.float32), np.sin(ang).astype(np.float32)
    return np.concatenate([c, c]), np.concatenate([s, -s])


def kernel(**inputs):
    import concourse.bacc as bacc
    from concourse.bass_utils import run_bass_kernel_spmd

    nc = bacc.Bacc("TRN2", target_bir_lowering=False, num_devices=1)
    arrays = {name: np.ascontiguousarray(inputs[name]) for name in _INS}
    arrays["rope_cos"], arrays["rope_sin"] = rotary_tables()
    dram = {name: nc.dram_tensor("in_" + name, a.shape, mybir.dt.from_np(a.dtype), kind="ExternalInput").ap()
            for name, a in arrays.items()}
    out = nc.dram_tensor("out_x", (S, D), F32, kind="ExternalOutput").ap()
    network(nc, dram, out)
    r = run_bass_kernel_spmd(nc, [{"in_" + name: a for name, a in arrays.items()}], core_ids=[0])
    return r.results[0]["out_x"].reshape(1, S, D)
```
